# Optimizing a Trainium2 kernel written in Bass

```python
import math
import jax, jax.numpy as jnp
from jax import lax
import numpy as np

D_MODEL = 1024
BATCH = 1
SEQ = 1024
DEPTH = 1

GRID_W = 64
CTX_LEN = 256
MLA_HEADS = 8
QK_NOPE = 64
QK_ROPE = 32
V_DIM = 64
Q_LORA = 256
KV_LORA = 128
ROPE_AXIS = QK_ROPE // 2
ROPE_BASE = 10000.0
Q_BLOCK = 128
ATTN_SCALE = (QK_NOPE + QK_ROPE) ** -0.5
POOL_WINDOWS = (2, 4, 8, 16)
POOL_GROUP = 64
POOL_WIDTH = POOL_GROUP * len(POOL_WINDOWS)
CONV_WIDTH = 256
CONV_K = 31
MLA_WIDTH = MLA_HEADS * V_DIM
MIX_WIDTH = MLA_WIDTH + POOL_WIDTH + CONV_WIDTH
OFF_KV = Q_LORA
OFF_KR = OFF_KV + KV_LORA
OFF_POOL = OFF_KR + QK_ROPE
OFF_CONV = OFF_POOL + POOL_WIDTH
IN_COLS = OFF_CONV + 2 * CONV_WIDTH
N_EXPERTS = 32
TOP_K = 4
N_GROUPS = 4
TOPK_GROUPS = 2
D_EXPERT = 256
D_SHARED = 256
ROUTED_SCALE = 2.5
ALPHA = (2 * DEPTH) ** 0.25
BETA = (8 * DEPTH) ** -0.25
EPS = 1e-6

kernel_name = 'hybrid_mla_pool_conv_moe_dit'

def _layernorm(x, g=None, b=None):
    x32 = x.astype(jnp.float32)
    mu = jnp.mean(x32, axis=-1, keepdims=True)
    var = jnp.mean(jnp.square(x32 - mu), axis=-1, keepdims=True)
    y = (x32 - mu) * lax.rsqrt(var + EPS)
    if g is not None:
        y = y * g + b
    return y.astype(x.dtype)

def _rmsnorm(x, g):
    x32 = x.astype(jnp.float32)
    y = x32 * lax.rsqrt(jnp.mean(jnp.square(x32), axis=-1, keepdims=True) + EPS)
    return (y * g).astype(x.dtype)

def _modulate(z, shift, scale):
    return _layernorm(z) * (1.0 + scale) + shift

def _post_norm(z, y, gate, g, b):
    return _layernorm(ALPHA * z + gate * y, g, b)

def _axial_tables(row, col):
    inv = ROPE_BASE ** (-jnp.arange(0, ROPE_AXIS, 2, dtype=jnp.float32) / ROPE_AXIS)
    ang_r = row.astype(jnp.float32)[:, None] * inv
    ang_c = col.astype(jnp.float32)[:, None] * inv
    return (jnp.cos(ang_r), jnp.sin(ang_r), jnp.cos(ang_c), jnp.sin(ang_c))

def _rotate(x, cos, sin):
    x1, x2 = jnp.split(x, 2, axis=-1)
    return jnp.concatenate([x1 * cos - x2 * sin, x2 * cos + x1 * sin], axis=-1)

def _rope_2d(x, tabs):
    cr, sr, cc, sc = (t.astype(x.dtype) for t in tabs)
    return jnp.concatenate([_rotate(x[..., :ROPE_AXIS], cr, sr),
                            _rotate(x[..., ROPE_AXIS:], cc, sc)], axis=-1)

def _mla_q(q_c, q_norm_g, w_uq):
    b, n, _ = q_c.shape
    q = (_rmsnorm(q_c, q_norm_g) @ w_uq).reshape(b, n, MLA_HEADS, QK_NOPE + QK_ROPE)
    return q[..., :QK_NOPE], q[..., QK_NOPE:]

def _mla_kv(kv_c, k_rope, kv_norm_g, w_ukv):
    b, n, _ = kv_c.shape
    kv = (_rmsnorm(kv_c, kv_norm_g) @ w_ukv).reshape(b, n, MLA_HEADS, QK_NOPE + V_DIM)
    return kv[..., :QK_NOPE], kv[..., QK_NOPE:], k_rope

def _latent_attention(qn, qr_rot, qr_raw, kn_all, v_all, kr_ctx, kr_lat):
    b, n, h, _ = qn.shape
    nb = n // Q_BLOCK

    def blocks(t):
        return jnp.swapaxes(t.reshape(b, nb, Q_BLOCK, h, t.shape[-1]), 0, 1)

    def one_block(args):
        qn_b, qrr_b, qr0_b = args
        s_nope = jnp.einsum('bqhd,bkhd->bhqk', qn_b, kn_all)
        s_rope = jnp.concatenate([
            jnp.einsum('bqhr,bkr->bhqk', qr0_b, kr_ctx),
            jnp.einsum('bqhr,bkr->bhqk', qrr_b, kr_lat)],
            axis=-1)
        p = jax.nn.softmax((s_nope + s_rope).astype(jnp.float32) * ATTN_SCALE, axis=-1)
        return jnp.einsum('bhqk,bkhd->bqhd', p.astype(v_all.dtype), v_all)

    o = lax.map(one_block, (blocks(qn), blocks(qr_rot), blocks(qr_raw)))
    return jnp.swapaxes(o, 0, 1).reshape(b, n, h * V_DIM)

def _context_attention(qn, qr, kn, kr, v):
    b, n = qn.shape[:2]
    s = jnp.einsum('bqhd,bkhd->bhqk', qn, kn) + jnp.einsum('bqhr,bkr->bhqk', qr, kr)
    p = jax.nn.softmax(s.astype(jnp.float32) * ATTN_SCALE, axis=-1)
    return jnp.einsum('bhqk,bkhd->bqhd', p.astype(v.dtype), v).reshape(b, n, MLA_WIDTH)

def _multiscale_pool(u, pool_w, pool_scale):
    b, n, ch = u.shape
    u32 = u.astype(jnp.float32)
    cs = jnp.concatenate([jnp.zeros((b, 1, ch), jnp.float32), jnp.cumsum(u32, axis=1)], axis=1)
    t = jnp.arange(n)
    outs = []
    for gi, w in enumerate(POOL_WINDOWS):
        lo = w // 2
        hi = w - 1 - lo
        start = jnp.clip(t - lo, 0, n)
        end = jnp.clip(t + hi + 1, 0, n)
        seg = cs[..., gi * POOL_GROUP:(gi + 1) * POOL_GROUP]
        mean = (jnp.take(seg, end, axis=1) - jnp.take(seg, start, axis=1)) / \
            (end - start).astype(jnp.float32)[None, :, None]
        diff = (mean - u32[..., gi * POOL_GROUP:(gi + 1) * POOL_GROUP]).astype(u.dtype)
        outs.append(diff @ pool_w[gi])
    return jnp.concatenate(outs, axis=-1) * pool_scale

def _conformer_conv(u2, conv_dw, conv_b, conv_ln_g, conv_ln_b, conv_pw):
    a, g = jnp.split(u2, 2, axis=-1)
    u = a * jax.nn.sigmoid(g)
    y = lax.conv_general_dilated(
        u, conv_dw[:, None, :], window_strides=(1,),
        padding=[(CONV_K // 2, CONV_K // 2)],
        dimension_numbers=('NWC', 'WIO', 'NWC'),
        feature_group_count=CONV_WIDTH) + conv_b
    y = jax.nn.silu(_layernorm(y, conv_ln_g, conv_ln_b))
    return y @ conv_pw

def _mix_out(att, p, pool_w, pool_scale, conv_dw, conv_b, conv_ln_g, conv_ln_b, conv_pw, w_out):
    pool = _multiscale_pool(p[..., OFF_POOL:OFF_CONV], pool_w, pool_scale)
    conv = _conformer_conv(p[..., OFF_CONV:], conv_dw, conv_b, conv_ln_g, conv_ln_b, conv_pw)
    return jnp.concatenate([att, pool, conv], axis=-1) @ w_out

def _swiglu(t, wg, wu, wd):
    return (jax.nn.silu(t @ wg) * (t @ wu)) @ wd

def _moe(h, router_w, router_bias, exp_wg, exp_wu, exp_wd, sh_wg, sh_wu, sh_wd):
    shape = h.shape
    t = h.reshape(-1, shape[-1])
    scores = jax.nn.sigmoid((t @ router_w).astype(jnp.float32))
    sel = scores + router_bias
    grp = sel.reshape(-1, N_GROUPS, N_EXPERTS // N_GROUPS)
    gscore = jnp.sum(lax.top_k(grp, 2)[0], axis=-1)
    _, gidx = lax.top_k(gscore, TOPK_GROUPS)
    gmask = jnp.sum(jax.nn.one_hot(gidx, N_GROUPS), axis=1) > 0
    emask = jnp.repeat(gmask, N_EXPERTS // N_GROUPS, axis=-1)
    _, eidx = lax.top_k(jnp.where(emask, sel, -jnp.inf), TOP_K)
    w = jnp.take_along_axis(scores, eidx, axis=-1)
    w = w / jnp.sum(w, axis=-1, keepdims=True) * ROUTED_SCALE
    gates = jnp.einsum('tk,tke->te', w, jax.nn.one_hot(eidx, N_EXPERTS)).astype(t.dtype)

    def add_expert(acc, xs):
        g_e, wg_e, wu_e, wd_e = xs
        return acc + g_e[:, None] * _swiglu(t, wg_e, wu_e, wd_e), None

    out, _ = lax.scan(add_expert, _swiglu(t, sh_wg, sh_wu, sh_wd),
                      (gates.T, exp_wg, exp_wu, exp_wd))
    return out.reshape(shape)

def setup_inputs(seed: int = 0) -> dict:
    key = jax.random.key(seed)
    ks = iter(jax.random.split(key, 40))
    L = DEPTH

    def nrm(shape, scale=1.0):
        return jax.random.normal(next(ks), shape, jnp.float32) * scale

    def gain(shape):
        return 1.0 + nrm(shape, 0.02)

    return {
        'x': nrm((BATCH, SEQ, D_MODEL)),
        'c': nrm((BATCH, D_MODEL)),
        'ctx': nrm((BATCH, CTX_LEN, D_MODEL)),
        'c_ctx': nrm((D_MODEL,)),
        'ada_w': nrm((L, D_MODEL, 6 * D_MODEL), 0.5 * D_MODEL ** -0.5),
        'ada_b': nrm((L, 6 * D_MODEL), 0.02),
        'w_in': nrm((L, D_MODEL, IN_COLS), D_MODEL ** -0.5),
        'q_norm_g': gain((L, Q_LORA)),
        'w_uq': nrm((L, Q_LORA, MLA_HEADS * (QK_NOPE + QK_ROPE)), Q_LORA ** -0.5),
        'kv_norm_g': gain((L, KV_LORA)),
        'w_ukv': nrm((L, KV_LORA, MLA_HEADS * (QK_NOPE + V_DIM)), KV_LORA ** -0.5),
        'pool_w': nrm((L, len(POOL_WINDOWS), POOL_GROUP, POOL_GROUP), POOL_GROUP ** -0.5),
        'pool_scale': gain((L, POOL_WIDTH)),
        'conv_dw': nrm((L, CONV_K, CONV_WIDTH), CONV_K ** -0.5),
        'conv_b': nrm((L, CONV_WIDTH), 0.02),
        'conv_ln_g': gain((L, CONV_WIDTH)),
        'conv_ln_b': nrm((L, CONV_WIDTH), 0.02),
        'conv_pw': nrm((L, CONV_WIDTH, CONV_WIDTH), CONV_WIDTH ** -0.5),
        'w_out': nrm((L, MIX_WIDTH, D_MODEL), BETA * MIX_WIDTH ** -0.5),
        'ln1_g': gain((L, D_MODEL)),
        'ln1_b': nrm((L, D_MODEL), 0.02),
        'router_w': nrm((L, D_MODEL, N_EXPERTS), D_MODEL ** -0.5),
        'router_bias': nrm((L, N_EXPERTS), 0.01),
        'exp_wg': nrm((L, N_EXPERTS, D_MODEL, D_EXPERT), D_MODEL ** -0.5),
        'exp_wu': nrm((L, N_EXPERTS, D_MODEL, D_EXPERT), D_MODEL ** -0.5),
        'exp_wd': nrm((L, N_EXPERTS, D_EXPERT, D_MODEL), BETA * D_EXPERT ** -0.5),
        'sh_wg': nrm((L, D_MODEL, D_SHARED), D_MODEL ** -0.5),
        'sh_wu': nrm((L, D_MODEL, D_SHARED), D_MODEL ** -0.5),
        'sh_wd': nrm((L, D_SHARED, D_MODEL), BETA * D_SHARED ** -0.5),
        'ln2_g': gain((L, D_MODEL)),
        'ln2_b': nrm((L, D_MODEL), 0.02),
    }

def reference(x, c, ctx, c_ctx, ada_w, ada_b, w_in, q_norm_g, w_uq, kv_norm_g, w_ukv,
              pool_w, pool_scale, conv_dw, conv_b, conv_ln_g, conv_ln_b, conv_pw, w_out,
              ln1_g, ln1_b, router_w, router_bias, exp_wg, exp_wu, exp_wd,
              sh_wg, sh_wu, sh_wd, ln2_g, ln2_b):
    n_lat = x.shape[1]
    n_rows = n_lat // GRID_W
    row = jnp.broadcast_to(jnp.arange(n_rows)[:, None], (n_rows, GRID_W)).reshape(-1)
    col = jnp.broadcast_to(jnp.arange(GRID_W)[None, :], (n_rows, GRID_W)).reshape(-1)
    tabs_k = _axial_tables(row, col)
    tabs_q = tuple(tb[:, None, :] for tb in tabs_k)

    zl, zc = x, ctx
    for l in range(DEPTH):
        last = l == DEPTH - 1
        mod_l = jnp.split((jax.nn.silu(c) @ ada_w[l] + ada_b[l])[:, None, :], 6, axis=-1)
        mod_c = jnp.split(jax.nn.silu(c_ctx) @ ada_w[l] + ada_b[l], 6, axis=-1)
        mix_p = (pool_w[l], pool_scale[l], conv_dw[l], conv_b[l], conv_ln_g[l],
                 conv_ln_b[l], conv_pw[l], w_out[l])
        moe_p = (router_w[l], router_bias[l], exp_wg[l], exp_wu[l], exp_wd[l],
                 sh_wg[l], sh_wu[l], sh_wd[l])

        pl = _modulate(zl, mod_l[0], mod_l[1]) @ w_in[l]
        hc = _modulate(zc, mod_c[0], mod_c[1])
        if last:
            pc_kv = hc @ w_in[l][:, OFF_KV:OFF_POOL]
        else:
            pc = hc @ w_in[l]
            pc_kv = pc[..., OFF_KV:OFF_POOL]
        kn_c, v_c, kr_c = _mla_kv(pc_kv[..., :KV_LORA], pc_kv[..., KV_LORA:],
                                  kv_norm_g[l], w_ukv[l])
        kn_l, v_l, kr_l = _mla_kv(pl[..., OFF_KV:OFF_KR], pl[..., OFF_KR:OFF_POOL],
                                  kv_norm_g[l], w_ukv[l])
        qn_l, qr_l = _mla_q(pl[..., :OFF_KV], q_norm_g[l], w_uq[l])
        att_l = _latent_attention(qn_l, _rope_2d(qr_l, tabs_q), qr_l,
                                  jnp.concatenate([kn_c, kn_l], axis=1),
                                  jnp.concatenate([v_c, v_l], axis=1),
                                  kr_c, _rope_2d(kr_l, tabs_k))
        zl = _post_norm(zl, _mix_out(att_l, pl, *mix_p), mod_l[2], ln1_g[l], ln1_b[l])
        zl = _post_norm(zl, _moe(_modulate(zl, mod_l[3], mod_l[4]), *moe_p),
                        mod_l[5], ln2_g[l], ln2_b[l])

        if not last:
            qn_c, qr_c = _mla_q(pc[..., :OFF_KV], q_norm_g[l], w_uq[l])
            att_c = _context_attention(qn_c, qr_c, kn_c, kr_c, v_c)
            zc = _post_norm(zc, _mix_out(att_c, pc, *mix_p), mod_c[2], ln1_g[l], ln1_b[l])
            zc = _post_norm(zc, _moe(_modulate(zc, mod_c[3], mod_c[4]), *moe_p),
                            mod_c[5], ln2_g[l], ln2_b[l])
    return zl


_drawn_inputs = setup_inputs


def setup_inputs(seed=0):
    import zlib

    import numpy as np

    out = dict(_drawn_inputs(seed))
    spreads = {}
    factors = {'ctx': 5.581,
     'c_ctx': 4.342,
     'q_norm_g': 8.0,
     'w_uq': 3.166,
     'kv_norm_g': 8.0,
     'pool_scale': 29.609,
     'conv_b': 7.883,
     'conv_ln_g': 110.221,
     'conv_ln_b': 87.567,
     'ln2_g': 25.817,
     'ln2_b': 23.949}
    for name, (base, spread) in spreads.items():
        noise = np.random.default_rng([zlib.crc32(name.encode()), seed]).standard_normal(out[name].shape)
        drawn = base * np.exp(spread * noise) if base else spread * noise
        out[name] = __import__('jax').numpy.asarray(drawn.astype(out[name].dtype))
    for name, factor in factors.items():
        out[name] = (out[name] * factor).astype(out[name].dtype)
    return out
```

```python
from contextlib import ExitStack

import numpy as np

import concourse.bass as bass
from concourse import mybir

F32 = mybir.dt.float32
I32 = mybir.dt.int32
BF16 = mybir.dt.bfloat16
ALU = mybir.AluOpType
ACT = mybir.ActivationFunctionType
AX = mybir.AxisListType

P = 128
D = 1024
KD = D // P
LT, CT = 8, 2
NT = LT + CT
SEQ, CTX = LT * P, CT * P
KEYS = SEQ + CTX
GRID_W = 64
HEADS, NOPE, ROPE, VD = 8, 64, 32, 64
HD = NOPE + ROPE
QL, KVL = 256, 128
QKV = QL + KVL + ROPE
POOL_W = (2, 4, 8, 16)
PG = 64
CW = 256
TAPS = 31
CPAD = TAPS // 2
PPAD = max(POOL_W) // 2
IN_COLS = QKV + CW + 2 * CW
SCALE = float(HD) ** -0.5
ALPHA = 2.0 ** 0.25
EPS = 1e-6
E = 32
GROUPS, GE = 4, 8
TOPK = 4
FE = 256
ROUTED_SCALE = 2.5
BLOCKS = SEQ * TOPK // P + E
HOTS = 8
BIG = 1e30

R_C, R_CC, R_MOD1, R_MOD2 = 0, 8, 16, 32
R_PSC, R_CB, R_LG, R_LB, R_QG, R_KVG, R_DW = 48, 50, 52, 54, 56, 58, 59
N_ROWS = R_DW + 2 * TAPS

C_ID, C_TRI, C_WINV, C_EDGE, C_IOTA = 0, 128, 256, 258, 290
C_TOK, C_GT, C_GE, C_COS, C_SIN = 322, 330, 346, 362, 490
C_POS, C_SPARE = 618, 746
N_CONST = 747


def shape_constants():
    t = np.zeros((P, N_CONST), np.float32)
    t[:, C_ID:C_ID + P] = np.eye(P)
    t[:, C_TRI:C_TRI + P] = np.triu(np.ones((P, P)), 1)
    for j in range(2):
        for s in range(2):
            w = POOL_W[2 * j + s]
            rows = slice(PG * s, PG * (s + 1))
            t[rows, C_WINV + j] = 1.0 / w
            pos = np.concatenate([np.arange(PPAD), np.arange(SEQ - PPAD, SEQ)])
            lo, hi = w // 2, w - 1 - w // 2
            n = np.clip(pos + hi + 1, 0, SEQ) - np.clip(pos - lo, 0, SEQ)
            t[rows, C_EDGE + 16 * j:C_EDGE + 16 * (j + 1)] = w / n
    t[:, C_IOTA:C_IOTA + E] = np.arange(E) - E
    t[:, C_TOK:C_TOK + LT] = np.arange(P)[:, None] + P * np.arange(LT)
    t[:, C_POS:C_POS + P] = np.arange(P)
    t[:, C_SPARE] = SEQ + np.arange(P)
    g, j = np.meshgrid(np.arange(GROUPS), np.arange(GROUPS), indexing="ij")
    t[:, C_GT:C_GT + 16] = (j > g).reshape(-1)
    t[:, C_GE:C_GE + 16] = (j < g).reshape(-1)
    axis = ROPE // 2
    inv = (np.float32(10000.0) ** (-np.arange(0, axis, 2, dtype=np.float32) / np.float32(axis))).astype(np.float32)
    tok = np.arange(SEQ)
    row, col = (tok // GRID_W).astype(np.float32), (tok % GRID_W).astype(np.float32)
    ang = np.concatenate([row[:, None] * inv, col[:, None] * inv], axis=1)
    for at, f in ((C_COS, np.cos), (C_SIN, np.sin)):
        t[:, at:at + 128] = f(ang).astype(np.float32).reshape(LT, P, 16).transpose(1, 0, 2).reshape(P, 128)
    return t


class Ring:

    def __init__(self):
        self.jobs, self.of, self.n = [], {}, {"act": 0, "dve": 0}

    def add(self, name, engine):
        self.n[engine] += 1
        self.of[name] = (len(self.jobs), engine, self.n[engine])
        self.jobs.append((name, engine))


def stage1_jobs():
    r = Ring()
    r.add(("rows",), "dve")
    groups = [(0, 2), (2, 6), (6, 10)]
    for g in range(3):
        for k in range(KD):
            r.add(("hT", g, k), "act" if k % 2 == 0 else "dve")
    for i in range(NT):
        r.add(("qkv", i), "act" if i % 2 == 0 else "dve")
    mixed = [("pool", j, n) for j in range(2) for n in range(2)]
    mixed += [(kind, j, n) for j in range(2) for n in range(2) for kind in ("cg", "ca")]
    gates = [("gate", m, q) for m in range(2) for q in range(4)]
    for m in mixed:
        r.add(m, "dve" if m[0] == "ca" else "act")
        if gates:
            r.add(gates.pop(0), "dve")
    for c in range(2):
        for n in range(2):
            r.add(("qcT", c, n), "act" if n else "dve")
    for g in range(3):
        r.add(("kvT", g), "act")
    for g in range(3):
        r.add(("krT", g), "dve")
    for i in range(NT):
        r.add(("V", i), "act" if i % 2 else "dve")
    return r, groups


UNITS = HEADS * LT
TAP_FIRST = 2
TAP_STEP = 46


def attention_slots():
    steps = [[] for _ in range(UNITS + 5)]
    for i in range(UNITS + 2):
        s = steps[i]
        if 1 <= i <= UNITS:
            s += [(("P", i - 1, 0), "a"), (("P", i - 1, 1), "b"), (("P", i - 1, 2), "a")]
        h, q = i // LT + 1, i % LT
        if h < HEADS and i < UNITS:
            s += sorted([(n, b) for n, b in prep_slots(h) if PREP_AT[n[0]][n[-1]] == q], key=lambda v: v[1] == "a")
    for p in range(HEADS // 2):
        at = 2 * LT * p + 2 * LT + 2
        steps[at] += [(("O", p, 0), "a"), (("O", p, 1), "b")]
    for n, at in ((0, 9), (1, 11), (2, 13), (3, 15)):
        steps[at].append((("pool", n // 2, n % 2), "b"))
    for s in range(4):
        steps[TAP_STEP + 1 + s].append((("y", s), "b"))
        steps[TAP_STEP + 9 + s].append((("yT", s // 2, s % 2), "a"))
    return steps


PREP_AT = {"q": (0, 1), "qraw": (3, 4), "qrot": (4, 5), "kn": (5, 6, 7)}


def prep_slots(h):
    if h > 0:
        return [((kind, h, n), "a" if (kind, n) in (("qraw", 1), ("kn", 0)) else "b")
                for kind, count in (("q", 2), ("qraw", 2), ("qrot", 2), ("kn", 3)) for n in range(count)]
    out = [(("q", h, n), "b" if n else "a") for n in range(2)]
    out += [(("qraw", h, n), "a" if n else "b") for n in range(2)]
    out += [(("qrot", h, n), "a" if n else "b") for n in range(2)]
    out += [(("kn", h, n), "ab"[n % 2]) for n in range(3)]
    return out


def build(nc, x, c, ctx, c_ctx, ada_w, ada_b, w_in, q_norm_g, w_uq, kv_norm_g, w_ukv, pool_w,
          pool_scale, conv_dw, conv_b, conv_ln_g, conv_ln_b, conv_pw, w_out, ln1_g, ln1_b,
          router_w, router_bias, exp_wg, exp_wu, exp_wd, sh_wg, sh_wu, sh_wd, ln2_g, ln2_b,
          const, zero_rows, out):
    with ExitStack() as stack:
        def sb(name, shape, dt=F32):
            return stack.enter_context(nc.sbuf_tensor(name, shape, dt))

        def sem(name):
            return stack.enter_context(nc.semaphore(name))

        zn_dram = nc.dram_tensor("zn_rows", [SEQ + P, D], F32, kind="Internal").ap()
        acc_dram = nc.dram_tensor("acc_rows", [SEQ + P, D], F32, kind="Internal").ap()

        LA, LB, LC, LD, LE, LF = 10240, 10240, 9472, 4864, 5184, 8192
        OA = 0
        OB = OA + LA
        OC = OB + LB
        OD = OC + LC
        OE = OD + LD
        OF = OE + LE
        arena = sb("arena", [P, OF + LF])

        def cut(at, n, *dims):
            v = arena[:, at:at + n]
            if len(dims) == 1:
                return v.rearrange("p (a b) -> p a b", a=dims[0])
            if len(dims) == 2:
                return v.rearrange("p (a b c) -> p a b c", a=dims[0], b=dims[1])
            return v

        xz = cut(OA, NT * D, NT)
        hT = cut(OB, KD * KEYS, KD)
        win = cut(OC, KD * IN_COLS, KD)
        ada_at = [OD, OD + 2048] + [OB + 2048 * n for n in range(5)] + [OF]
        ada = [cut(at, KD * 256, KD) for at in ada_at]
        sig = cut(OA + 5120, 1024, 2)
        junk = cut(OA + 4608, 256)
        qkv = cut(OE, NT * QKV, NT)
        ada_acc = cut(OE + NT * QKV, 3 * 256, 3)
        mrow = cut(OE, 2 * D)
        ada_ones = cut(OE + NT * QKV + 3 * 256, P)
        qcT = cut(OF, 2 * SEQ, 2)
        kvT = cut(OF + 2048, KEYS)
        wuq = cut(OF + 3328, 2 * HEADS * HD, 2)
        wukv = cut(OF + 4864, D)
        uconv = cut(OF + 5888, 2 * (SEQ + 2 * CPAD), 2)
        upool = cut(OA, 2 * (SEQ + 2 * PPAD), 2)
        ptmp = cut(OA + 2080, 2 * (SEQ + 2 * PPAD), 2)
        mixT = cut(OA, KD * SEQ, KD)
        pdif = cut(OA + 6 * SEQ, 2 * SEQ, 2)
        yconv = cut(OA + KD * SEQ, 2 * SEQ, 2)
        KT = cut(OB, 2 * KEYS, 2)
        QT = cut(OB + 2560, 4 * SEQ, 2, 2)
        probs = cut(OB + 6656, 2 * KEYS, 2)
        Opair = [cut(OC + 8192, SEQ, LT), cut(OB + 9216, SEQ, LT)]
        wout = cut(OC, KD * D, KD)
        probsT = cut(OD, 2 * KEYS, 2, NT)
        qraw = cut(OD + 2560, 2 * LT * HD, 2, LT)
        qrot = cut(OD + 4096, LT * HD, LT)
        V = cut(OE, NT * HEADS * VD, NT)
        ytok = cut(OF + 5888, LT * CW, LT)
        z1 = cut(OB, LT * D, LT)
        ln_rows = cut(OB + LT * D, 2 * D, 2)
        slot0 = OD
        zst = cut(OD + 6144, 2 * D, 2)
        ztmp = cut(OD + 8192, D)
        silS = cut(OD + 9216, 512)
        hmS = cut(OA + 8192, 2 * 512, 2)
        h2T = cut(OF, KD * SEQ, KD)
        slots = [slot0, OA, OC + 2048, OF]
        wg = [cut(s, 2048, KD) for s in slots]
        wu = [cut(s + 2048, 2048, KD) for s in slots]
        wd = [cut(s + 4096, 2048, 2) for s in slots]
        xe = cut(OA + 6144, D)
        xeT = cut(OA + 7168, D, KD)
        ye = cut(OA + 8192, D)
        hmE = cut(OA + 9216, 256, 2)
        silE = cut(OA + 9472, 256, 2)
        ln2_rows = cut(OC, 2 * D, 2)
        chosen = cut(OA + 6144, TOPK * LT * E, TOPK, LT)
        score = cut(OA + 7168, LT * E, LT)
        sel = cut(OA + 7424, LT * E, LT)
        rt = cut(OA + 7680, LT * E, LT)
        member = arena[:, OA + 7936:OA + 7936 + LT * E // 2].bitcast(BF16).rearrange("p (t e) -> p t e", t=LT)
        small = cut(OB + LT * D, 512, 16)
        nb_tab = sb("nb_tab", [P, 2 * E + 1], I32)
        weight = sb("weight", [P, TOPK, LT])
        NB = BLOCKS + 2
        place_hot = cut(OD + 6144, HOTS * P, HOTS)
        block_hot = cut(OB + LT * D + 512, HOTS * 2 * NB, HOTS)
        logitsT = arena[0:E, OA + 9216:OA + 9216 + SEQ]
        exact = arena[:, OC + 8192:OC + 8192 + P].bitcast(BF16)
        ids = sb("ids", [P, NB], I32)
        wts = sb("wts", [P, NB])
        id_in, id_out, w_now = sb("id_in", [P, 1], I32), sb("id_out", [P, 1], I32), sb("w_now", [P, 1])
        rw = sb("rw", [P, KD, E])
        rb = sb("rb", [P, E])
        pw = cut(OD + 6144, 2 * CW, 2)

        cst = sb("cst", [P, N_CONST])
        rows = sb("rows", [P, P])
        col = sb("col", [P, N_ROWS])
        sc = sb("sc", [P, 16])
        mod1 = sb("mod1", [P, 2, KD, 2])
        mod2 = sb("mod2", [P, 2, KD])
        gates = sb("gates", [P, 2, D])
        stats = sb("stats", [P, 2, 6])
        mv = sb("mv", [P, NT, 2])
        rstd = sb("rstd", [P, NT])
        ssq = sb("ssq", [P, NT, 2])
        rq = sb("rq", [P, NT, 2])
        mhalf = sb("mhalf", [P, 2 * NT])
        rtmp = sb("rtmp", [P, 4, 128])
        nmax = sb("nmax", [P, 4])
        rsum = sb("rsum", [P, 4])
        rinv = sb("rinv", [P, 2])
        bdiag = sb("bdiag", [P, 2, P])
        mark = sb("mark", [P, 2])
        ones_t = rtmp[:, 0, :]
        psum = stack.enter_context(nc.psum_tensor("psum", [P, 8 * 512], F32))

        def bank(b, n=512, at=0):
            return psum[:, b * 512 + at:b * 512 + at + n]

        ident = cst[:, C_ID:C_ID + P]

        ring, groups = stage1_jobs()
        slots_at = attention_slots()

        consts_in, rows_in, x_in = sem("consts_in"), sem("rows_in"), [sem(f"x_in{g}") for g in range(3)]
        ada_in = [sem(f"ada_in{n}") for n in range(8)]
        win_in, win2_in, gates_in, wq_in, wout_in = sem("win_in"), sem("win2_in"), sem("gates_in"), sem("wq_in"), sem("wout_in")
        job_done = sem("job_done")
        emptied = {"act": sem("emptied_act"), "dve": sem("emptied_dve")}
        ada_used = sem("ada_used")
        ada_summed = sem("ada_summed")
        mod_sum = sem("mod_sum")
        mod_rows = sem("mod_rows")
        mod_ready = sem("mod_ready")
        silu_ready = sem("silu_ready")
        var_ready, rstd_ready, z_ready = sem("var_ready"), sem("rstd_ready"), sem("z_ready")
        ssq_ready, rq_ready, lat_ready = sem("ssq_ready"), sem("rq_ready"), sem("lat_ready")
        kr_ready = sem("kr_ready")
        dve_step, act_step, pool_step = sem("dve_step"), sem("act_step"), sem("pool_step")
        pads_ready, zeros_ready, diag_in = sem("pads_ready"), sem("zeros_ready"), sem("diag_in")
        pdif_ready = sem("pdif_ready")
        scores_ready, nmax_ready, probs_ready = sem("scores_ready"), sem("nmax_ready"), sem("probs_ready")
        filled = {"a": sem("filled_a"), "b": sem("filled_b")}
        cleared = {"a": sem("cleared_a"), "b": sem("cleared_b")}
        O_ready, O_kept = sem("O_ready"), sem("O_kept")
        rope_ready = sem("rope_ready")
        conv_ready, ytok_ready = sem("conv_ready"), sem("ytok_ready")
        stored = sem("stored")

        SLOT_BANK = {"a": 5, "b": 6}
        slot_no, n_slots = {}, {"a": 0, "b": 0}
        for name, b in prep_slots(0):
            n_slots[b] += 1
            slot_no[name] = (b, n_slots[b])
        for s in slots_at:
            for name, b in s:
                n_slots[b] += 1
                slot_no[name] = (b, n_slots[b])

        def job_emptied(eng, name):
            _, e, n = ring.of[name]
            eng.wait_ge(emptied[e], n)

        def slot_cleared(eng, name):
            b, n = slot_no[name]
            eng.wait_ge(cleared[b], n)

        def chain(eng, s, count, ins):
            count[0] += 1
            ins.then_inc(s, 1)
            eng.wait_ge(s, count[0])

        block = stack.enter_context(nc.Block())

        ADA_PIECES = [("col", 0, q) for q in range(8)] + [("gate", m, q) for m in range(2) for q in range(4)] \
            + [("col", 1, q) for q in range(8)]
        def ada_col(p):
            kind, m, q = p
            if kind == "col":
                return 3 * D * m + 256 * q
            return (2 * D if m == 0 else 5 * D) + 256 * q

        RV = lambda v, n: v.rearrange("(r q) -> r q", q=P)

        misc_in, pw_in = sem("misc_in"), sem("pw_in")
        x2_in = [sem(f"x2_in{t}") for t in range(LT)]
        ln1_in, shared_in, ln2_in, fills_in = sem("ln1_in"), sem("shared_in"), sem("ln2_in"), sem("fills_in")
        yact_ready, pw_done, pw_kept = sem("yact_ready"), sem("pw_done"), sem("pw_kept")
        proj_done, proj_used = sem("proj_done"), sem("proj_used")
        var3, rstd3, norm3, gain3, zst_ready = (sem(n) for n in ("var3", "rstd3", "norm3", "gain3", "zst_ready"))
        zn_out = [sem("zn_out0"), sem("zn_out1")]
        zT_done, zT_kept = sem("zT_done"), sem("zT_kept")
        up_done, sil_ready, hm_ready = sem("up_done"), sem("sil_ready"), sem("hm_ready")
        down_done, down_used, acc_out = sem("down_done"), sem("down_used"), sem("acc_out")
        logits_done, score_ready, member_ready, pos_done, slots_ready = (
            sem(n) for n in ("logits_done", "score_ready", "member_ready", "pos_done", "slots_ready"))
        logitsT_done, logitsT_kept, exact_ready = (sem(n) for n in ("logitsT_done", "logitsT_kept", "exact_ready"))
        hot_ready, hot_used, ids_ready = (sem(n) for n in ("hot_ready", "hot_used", "ids_ready"))
        weights_in = [sem(f"weights_in{n}") for n in range(4)]
        gathered, xT_done, xT_act, xT_dve = (sem(n) for n in ("gathered", "xT_done", "xT_act", "xT_dve"))
        eup_done, esil, ehm, edown, y_ready, scattered, w_ready = (
            sem(n) for n in ("eup_done", "esil", "ehm", "edown", "y_ready", "scattered", "w_ready"))
        id_step = sem("id_step")
        acc_in = [sem(f"acc_in{t}") for t in range(LT)]
        var5, rstd5, norm5, final_ready = (sem(n) for n in ("var5", "rstd5", "norm5", "final_ready"))

        HALVES = [slice(0, 512), slice(512, D)]

        def stage3_loads(sp):
            sp.dma_start(rw[:, :, :], router_w.rearrange("(k p) e -> p k e", p=P)).then_inc(misc_in, 16)
            sp.dma_start(rb[:, :], router_bias.partition_broadcast(P)).then_inc(misc_in, 16)
            sp.dma_start(zn_dram[SEQ:SEQ + P, :], zero_rows).then_inc(fills_in, 16)
            sp.dma_start(acc_dram[SEQ:SEQ + P, :], zero_rows).then_inc(fills_in, 16)
            for b in "ab":
                sp.wait_ge(filled[b], n_slots[b])
            sp.wait_ge(probs_ready, UNITS)
            sp.dma_start(pw, conv_pw.rearrange("(k p) f -> p k f", p=P)).then_inc(pw_in, 16)
            for t in range(LT):
                sp.dma_start(z1[:, t, :], x[0, t * P:(t + 1) * P, :]).then_inc(x2_in[t], 16)
                if t == 0:
                    sp.dma_start(ln_rows[:, 0, :], ln1_g.partition_broadcast(P)).then_inc(ln1_in, 16)
                    sp.dma_start(ln_rows[:, 1, :], ln1_b.partition_broadcast(P)).then_inc(ln1_in, 16)
            for dst, src in ((wg[0], sh_wg), (wu[0], sh_wu), (wd[0], sh_wd)):
                sp.dma_start(dst, src.rearrange("(k p) f -> p k f", p=P)).then_inc(shared_in, 16)
            for t in range(LT):
                sp.wait_ge(zst_ready, t + 1)
                sp.dma_start(zn_dram[t * P:(t + 1) * P, :], zst[:, t % 2, :]).then_inc(zn_out[t % 2], 16)

            def expert(e, slot):
                for dst, src in ((wg[slot], exp_wg), (wu[slot], exp_wu), (wd[slot], exp_wd)):
                    sp.dma_start(dst, src[e].rearrange("(k p) f -> p k f", p=P)).then_inc(weights_in[slot], 16)

            sp.wait_ge(proj_done, LT)
            expert(0, 1)
            expert(1, 2)
            sp.dma_start(ln2_rows[:, 0, :], ln2_g.partition_broadcast(P)).then_inc(ln2_in, 16)
            sp.dma_start(ln2_rows[:, 1, :], ln2_b.partition_broadcast(P)).then_inc(ln2_in, 16)
            for t in range(LT):
                if t == 4:
                    sp.wait_ge(up_done, 4)
                    expert(2, 3)
                sp.wait_ge(down_used, 2 * t + 2)
                sp.dma_start(acc_dram[t * P:(t + 1) * P, :], z1[:, t, :]).then_inc(acc_out, 16)
            sp.wait_ge(down_done, 2 * LT)
            expert(3, 0)
            with sp.Fori(1, E // 4) as g:
                for s in range(4):
                    before = sp.value_load(nb_tab[0:1, bass.ds(E + 4 * (g - 1) + s + 1, 1)], min_val=1, max_val=BLOCKS)
                    sp.wait_ge(edown, before)
                    expert(4 * g + s, (s + 1) % 4)
            total = sp.value_load(nb_tab[0:1, 2 * E:2 * E + 1], min_val=1, max_val=BLOCKS)
            sp.wait_ge(scattered, total * 16 + 16)
            for t in range(LT):
                sp.dma_start(z1[:, t, :], acc_dram[t * P:(t + 1) * P, :]).then_inc(acc_in[t], 16)
            for t in range(LT):
                sp.wait_ge(final_ready, t + 1)
                sp.dma_start(out[0, t * P:(t + 1) * P, :], z1[:, t, :]).then_inc(stored, 16)
            sp.wait_ge(stored, 16 * LT)

        def stage3_tensor(pe):
            pe.wait_ge(pw_in, 16)
            pe.wait_ge(yact_ready, 1)
            for j in range(2):
                for n in range(2):
                    for k in range(2):
                        mm = nc.tensor.matmul(bank(2 * j + n), pw[:, k, j * P:(j + 1) * P], yconv[:, k, HALVES[n]],
                                              start=k == 0, stop=k == 1)
                    mm.then_inc(pw_done, 1)
            pe.wait_ge(wout_in, 16)
            for b in "ab":
                pe.wait_ge(cleared[b], n_slots[b])
            pe.wait_ge(pw_kept, 4)

            def project(i):
                b0 = 2 * (i % 2)
                if i >= 2:
                    pe.wait_ge(proj_used, i - 1)
                for h in range(2):
                    for k in range(KD):
                        mm = nc.tensor.matmul(bank(b0 + h), mixT[:, k, i * P:(i + 1) * P], wout[:, k, HALVES[h]],
                                              start=k == 0, stop=k == KD - 1)
                mm.then_inc(proj_done, 1)

            def turn(i):
                pe.wait_ge(zst_ready, i + 1)
                if i >= 1:
                    pe.wait_ge(zT_kept, i)
                for k in range(KD):
                    mm = nc.tensor.transpose(bank(5 + k // 4, P, (k % 4) * P), zst[:, i % 2, k * P:(k + 1) * P], ident)
                mm.then_inc(zT_done, 1)

            for i in range(LT):
                project(i)
                if i >= 1:
                    turn(i - 1)

            def shared_up(n, f):
                if n == 1:
                    pe.wait_ge(hm_ready, f + 1)
                for m, w in ((0, wg[0]), (1, wu[0])):
                    for k in range(KD):
                        mm = nc.tensor.matmul(bank(2 * f + m), w[:, k, f * P:(f + 1) * P], h2T[:, k, HALVES[n]],
                                              start=k == 0, stop=k == KD - 1)
                mm.then_inc(up_done, 1)

            def shared_down(n):
                pe.wait_ge(hm_ready, 2 * n + 2)
                for t in range(4):
                    for h in range(2):
                        q = 8 * n + 2 * t + h
                        if q >= 3:
                            pe.wait_ge(down_used, q - 2)
                        for k in range(2):
                            mm = nc.tensor.matmul(bank(4 + q % 3), hmS[:, k, t * P:(t + 1) * P], wd[0][:, k, HALVES[h]],
                                                  start=k == 0, stop=k == 1)
                        mm.then_inc(down_done, 1)

            def logits(n):
                if n == 0:
                    pe.wait_ge(misc_in, 32)
                else:
                    pe.wait_ge(logitsT_kept, 1)
                for k in range(KD):
                    mm = nc.tensor.matmul(bank(7)[0:E, :], rw[:, k, :], h2T[:, k, HALVES[n]], start=k == 0, stop=k == KD - 1)
                mm.then_inc(logitsT_done, 1)

            pe.wait_ge(shared_in, 48)
            pe.wait_ge(proj_used, LT)
            pe.wait_ge(zT_kept, 7)
            shared_up(0, 0)
            shared_up(0, 1)
            shared_down(0)
            pe.wait_ge(down_used, 8)
            turn(LT - 1)
            logits(0)
            pe.wait_ge(zT_kept, LT)
            logits(1)
            pe.wait_ge(logitsT_kept, 2)
            for i in range(LT):
                mm = nc.tensor.transpose(bank(7, E, i * E), logitsT[:, i * P:(i + 1) * P], ident[0:E, 0:E])
            mm.then_inc(logits_done, 1)
            shared_up(1, 0)
            pe.wait_ge(member_ready, 1)
            pe.wait_ge(exact_ready, 1)
            tri, ones = exact[:, 0:P], exact[:, P:2 * P]
            for i in range(LT):
                for j in range(i + 1):
                    nc.tensor.matmul(bank(7, E, i * E), tri if j == i else ones, member[:, j, :], start=j == 0, stop=j == i)
            for j in range(LT):
                mm = nc.tensor.matmul(bank(7, E, LT * E), ones, member[:, j, :], start=j == 0, stop=j == LT - 1)
            mm.then_inc(pos_done, 1)
            shared_up(1, 1)
            for n in range(TOPK * LT):
                pe.wait_ge(hot_ready, n + 1)
                nc.tensor.matmul(bank(7, 2 * NB), place_hot[:, n % HOTS, :], block_hot[:, n % HOTS, :],
                                 start=n == 0, stop=n == TOPK * LT - 1).then_inc(hot_used, 1)
            shared_down(1)

            def turn_rows():
                for k in range(KD):
                    mm = nc.tensor.transpose(bank(2 + k // 4, P, (k % 4) * P), xe[:, k * P:(k + 1) * P], ident)
                mm.then_inc(xT_done, 1)

            pe.wait_ge(gathered, 16)
            turn_rows()
            with pe.Fori(0, E // 4) as g:
                for s in range(4):
                    slot = (s + 1) % 4
                    pe.wait_ge(weights_in[slot], g * 48 + 48)
                    n = pe.value_load(nb_tab[0:1, bass.ds(4 * g + s, 1)], min_val=1, max_val=LT)
                    first = pe.value_load(nb_tab[0:1, bass.ds(E + 4 * g + s, 1)], min_val=0, max_val=BLOCKS - 1)
                    with pe.Fori(0, n) as j:
                        pe.wait_ge(xT_act, first + j + 1)
                        pe.wait_ge(xT_dve, first + j + 1)
                        for f in range(2):
                            for m, w in ((0, wg[slot]), (1, wu[slot])):
                                for k in range(KD):
                                    mm = nc.tensor.matmul(bank(f, P, m * P), w[:, k, f * P:(f + 1) * P], xeT[:, k, :],
                                                          start=k == 0, stop=k == KD - 1)
                            mm.then_inc(eup_done, 1)
                        pe.wait_ge(gathered, (first + j) * 16 + 32)
                        turn_rows()
                        for k in range(2):
                            pe.wait_ge(ehm, (first + j) * 2 + k + 1)
                            for h in range(2):
                                mm = nc.tensor.matmul(bank(4 + h), hmE[:, k, :], wd[slot][:, k, HALVES[h]],
                                                      start=k == 0, stop=k == 1)
                        mm.then_inc(edown, 1)

        def stage3_scalar(act):
            for j in range(2):
                slot_cleared(act, ("yT", j, 0))
                slot_cleared(act, ("yT", j, 1))
            nc.scalar.activation(yconv, yconv, ACT.Silu).then_inc(yact_ready, 1)
            for j in range(2):
                for n in range(2):
                    act.wait_ge(pw_done, 2 * j + n + 1)
                    nc.scalar.copy(mixT[:, 6 + j, HALVES[n]], bank(2 * j + n)).then_inc(pw_kept, 1)

            def keep_turn(i):
                act.wait_ge(zT_done, i + 1)
                for k in range(KD):
                    ins = nc.scalar.activation(h2T[:, k, i * P:(i + 1) * P], bank(5 + k // 4, P, (k % 4) * P), ACT.Identity,
                                               bias=mod2[:, 0, k:k + 1], scale=mod2[:, 1, k:k + 1])
                ins.then_inc(zT_kept, 1)

            def gate(n):
                for f in range(2):
                    act.wait_ge(up_done, 2 * n + f + 1)
                    if 2 * n + f >= 1:
                        act.wait_ge(hm_ready, 2 * n + f)
                    nc.scalar.activation(silS, bank(2 * f), ACT.Silu).then_inc(sil_ready, 1)

            for i in range(LT - 1):
                keep_turn(i)
            gate(0)
            keep_turn(LT - 1)
            for n in range(2):
                act.wait_ge(logitsT_done, n + 1)
                nc.scalar.copy(logitsT[:, HALVES[n]], bank(7)[0:E, :]).then_inc(logitsT_kept, 1)
            act.wait_ge(logits_done, 1)
            nc.scalar.activation(score.rearrange("p t e -> p (t e)"), bank(7, LT * E), ACT.Sigmoid).then_inc(score_ready, 1)
            gate(1)

            def keep_rows():
                for k in range(4, KD):
                    ins = nc.scalar.activation(xeT[:, k, :], bank(3, P, (k - 4) * P), ACT.Identity,
                                               bias=mod2[:, 0, k:k + 1], scale=mod2[:, 1, k:k + 1])
                ins.then_inc(xT_act, 1)

            act.wait_ge(ids_ready, 1)
            total = act.value_load(nb_tab[0:1, 2 * E:2 * E + 1], min_val=1, max_val=BLOCKS)
            act.wait_ge(xT_done, 1)
            keep_rows()
            with act.Fori(0, total) as b:
                for f in range(2):
                    act.wait_ge(eup_done, b * 2 + f + 1)
                    nc.scalar.activation(silE[:, f, :], bank(f, P), ACT.Silu).then_inc(esil, 1)
                act.wait_ge(xT_done, b + 2)
                keep_rows()

        def stage3_vector(dve, then):
            dve.wait_ge(ln1_in, 32)
            for i in range(LT):
                z = z1[:, i, :]
                dve.wait_ge(proj_done, i + 1)
                nc.vector.tensor_tensor(ztmp, psum[:, 1024 * (i % 2):1024 * (i % 2) + D], gates[:, 0, :], ALU.mult)\
                    .then_inc(proj_used, 1)
                dve.wait_ge(proj_used, i + 1)
                dve.wait_ge(x2_in[i], 16)
                then(nc.vector.scalar_tensor_tensor(z, z, ALPHA, ztmp, ALU.mult, ALU.add))
                for part in range(2):
                    if part:
                        dve.wait_ge(gain3, i + 1)
                    for s in range(2):
                        then(nc.vector.bn_stats(stats[:, s, :], z[:, s * 512:(s + 1) * 512]))
                    nc.vector.bn_aggr(mv[:, i, :], stats[:, :, :].rearrange("p a b -> p (a b)")).then_inc(var3, 1)
                    dve.wait_ge(rstd3, 2 * i + part + 1)
                    if part == 0:
                        nc.vector.tensor_scalar(z, z, mv[:, i, 0:1], rstd[:, i:i + 1], ALU.subtract, ALU.mult).then_inc(norm3, 1)
                    else:
                        if i >= 2:
                            dve.wait_ge(zn_out[i % 2], 16 * (i // 2))
                            dve.wait_ge(zT_done, i - 1)
                        nc.vector.tensor_scalar(zst[:, i % 2, :], z, mv[:, i, 0:1], rstd[:, i:i + 1],
                                                ALU.subtract, ALU.mult).then_inc(zst_ready, 1)

            def hidden(n, f):
                if n == 1 and f == 0:
                    dve.wait_ge(down_done, 8)
                dve.wait_ge(sil_ready, 2 * n + f + 1)
                nc.vector.tensor_tensor(hmS[:, f, :], bank(2 * f + 1), silS, ALU.mult).then_inc(hm_ready, 1)

            def start_sums(n):
                for t in range(4):
                    for h in range(2):
                        q = 8 * n + 2 * t + h
                        dve.wait_ge(down_done, q + 1)
                        z = z1[:, 4 * n + t, HALVES[h]]
                        then(nc.vector.tensor_tensor(ztmp[:, HALVES[h]], bank(4 + q % 3), gates[:, 1, HALVES[h]], ALU.mult))
                        nc.vector.scalar_tensor_tensor(z, z, ALPHA, ztmp[:, HALVES[h]], ALU.mult, ALU.add).then_inc(down_used, 1)

            hidden(0, 0)
            hidden(0, 1)
            start_sums(0)

            V = nc.vector
            tt, ts, stt, red = V.tensor_tensor, V.tensor_scalar, V.scalar_tensor_tensor, V.tensor_reduce
            S = lambda n: small[:, n, :]
            S8 = lambda n, m=0: small[:, n, 8 * m:8 * m + 8]
            by_group = lambda v: v.rearrange("p t (g e) -> p (t g) e", g=GROUPS)
            over8 = lambda v: v.unsqueeze(2).to_broadcast([P, 32, GE])
            over32 = lambda v: v.unsqueeze(2).to_broadcast([P, LT, E])
            dve.wait_ge(score_ready, 1)
            then(tt(sel, score, rb[:, :].unsqueeze(1).to_broadcast([P, LT, E]), ALU.add))
            then(red(S(0), by_group(sel), AX.X, ALU.max))
            then(tt(by_group(rt), by_group(sel), over8(S(0)), ALU.is_equal))
            then(red(S(1), by_group(rt), AX.X, ALU.add))
            then(stt(by_group(rt), by_group(rt), -BIG, by_group(sel), ALU.mult, ALU.add))
            then(red(S(2), by_group(rt), AX.X, ALU.max))
            then(ts(S(1), S(1), 1.5, 1.0, ALU.is_gt, ALU.subtract))
            then(stt(S(1), S(1), BIG, S(0), ALU.mult, ALU.add))
            then(tt(S(2), S(2), S(1), ALU.max))
            then(tt(S(3), S(0), S(2), ALU.add))
            gs = S(3).rearrange("p (t g) -> p t g", g=GROUPS)
            other = gs.unsqueeze(2).to_broadcast([P, LT, GROUPS, GROUPS])
            own = gs.unsqueeze(3).to_broadcast([P, LT, GROUPS, GROUPS])
            grid = lambda v: v.rearrange("p (t g j) -> p t g j", t=LT, g=GROUPS)
            ga = rt.rearrange("p t e -> p (t e)")[:, 0:128]
            gb = rt.rearrange("p t e -> p (t e)")[:, 128:256]
            mask = lambda at: cst[:, at:at + 16].unsqueeze(1).to_broadcast([P, LT, 16])
            flat = lambda v: v.rearrange("p (t g) -> p t g", t=LT)
            then(tt(grid(ga), other, own, ALU.is_gt))
            then(tt(grid(gb), other, own, ALU.is_ge))
            then(tt(flat(ga), flat(ga), mask(C_GT), ALU.mult))
            then(tt(flat(gb), flat(gb), mask(C_GE), ALU.mult))
            then(tt(ga, ga, gb, ALU.add))
            then(red(S(1), ga.rearrange("p (g j) -> p g j", j=GROUPS), AX.X, ALU.add))
            then(ts(S(1), S(1), 1.5, 1.0, ALU.is_lt, ALU.subtract))
            then(stt(by_group(sel), over8(S(1)), BIG, by_group(sel), ALU.mult, ALU.add))
            iota = cst[:, C_IOTA:C_IOTA + E].unsqueeze(1).to_broadcast([P, LT, E])
            for k in range(TOPK):
                then(red(S8(4), sel, AX.X, ALU.max))
                then(tt(rt, sel, over32(S8(4)), ALU.is_equal))
                then(tt(rt, rt, iota, ALU.mult))
                then(red(S8(4, 1), rt, AX.X, ALU.min))
                then(tt(chosen[:, k], iota, over32(S8(4, 1)), ALU.is_equal))
                then(stt(sel, chosen[:, k], -BIG, sel, ALU.mult, ALU.add))
            then(tt(member, chosen[:, 0], chosen[:, 1], ALU.add))
            then(tt(rt, chosen[:, 2], chosen[:, 3], ALU.add))
            tt(member, member, rt, ALU.add).then_inc(member_ready, 1)
            dve.wait_ge(member_ready, 1)
            for k in range(TOPK):
                then(tt(rt, chosen[:, k], score, ALU.mult))
                then(red(S8(5, k), rt, AX.X, ALU.add))
            then(red(S8(6), S(5).rearrange("p (k t) -> p t k", k=TOPK), AX.X, ALU.add))
            then(V.reciprocal(S8(6, 1), S8(6)))
            then(ts(S8(6, 1), S8(6, 1), ROUTED_SCALE, None, ALU.mult))
            then(tt(weight[:, :, :], S(5).rearrange("p (k t) -> p k t", k=TOPK),
                    S8(6, 1).unsqueeze(1).to_broadcast([P, TOPK, LT]), ALU.mult))
            hidden(1, 0)
            dve.wait_ge(pos_done, 1)
            si = small[:, 7, :].bitcast(I32)
            then(ts(si, bank(7, E, LT * E), float(P - 1), None, ALU.add))
            then(ts(si, si, 7, None, ALU.logical_shift_right))
            then(ts(nb_tab[:, 0:E], si, 1, None, ALU.max))
            then(V.tensor_copy(S(8), nb_tab[:, 0:E]))
            then(V.tensor_copy(S(9), S(8)))
            a, b = 9, 10
            for d in (1, 2, 4, 8, 16):
                then(V.tensor_copy(S(b)[:, 0:d], S(a)[:, 0:d]))
                then(tt(S(b)[:, d:E], S(a)[:, d:E], S(a)[:, 0:E - d], ALU.add))
                a, b = b, a
            then(V.tensor_copy(nb_tab[:, 2 * E:2 * E + 1], S(a)[:, E - 1:E]))
            then(tt(S(11), S(a), S(8), ALU.subtract))
            then(V.tensor_copy(nb_tab[:, E:2 * E], S(11)))
            then(stt(sel, S(11).unsqueeze(1).to_broadcast([P, LT, E]), float(P),
                     bank(7, LT * E).rearrange("p (t e) -> p t e", e=E), ALU.mult, ALU.add))
            for k in range(TOPK):
                then(tt(rt, chosen[:, k], sel, ALU.mult))
                then(red(S8(12, k), rt, AX.X, ALU.add))
            place_i, blk_i = small[:, 13, :].bitcast(I32), small[:, 14, :].bitcast(I32)
            place, blk, token = 9, 10, 15
            then(V.tensor_copy(si, S(12)))
            then(ts(place_i, si, P - 1, None, ALU.bitwise_and))
            then(ts(blk_i, si, 7, None, ALU.logical_shift_right))
            then(V.tensor_copy(S(place), place_i))
            then(V.tensor_copy(S(blk), blk_i))
            tok = cst[:, C_TOK:C_TOK + LT].unsqueeze(1).to_broadcast([P, TOPK, LT])
            stt(S(token).rearrange("p (k t) -> p k t", k=TOPK), S(place).rearrange("p (k t) -> p k t", k=TOPK),
                float(SEQ), tok, ALU.add, ALU.subtract).then_inc(slots_ready, 1)
            dve.wait_ge(slots_ready, 1)
            for z in zn_out:
                dve.wait_ge(z, 64)
            dve.wait_ge(zT_done, LT)
            w_flat = weight[:, :, :].rearrange("p k t -> p (k t)")
            for n in range(TOPK * LT):
                if n >= HOTS:
                    dve.wait_ge(hot_used, n - HOTS + 1)
                ts(place_hot[:, n % HOTS, :], cst[:, C_POS:C_POS + P], S(place)[:, n:n + 1], None, ALU.is_equal)
                ts(block_hot[:, n % HOTS, 0:NB], cst[:, C_POS:C_POS + NB], S(blk)[:, n:n + 1], S(token)[:, n:n + 1],
                   ALU.is_equal, ALU.mult)
                ts(block_hot[:, n % HOTS, NB:2 * NB], cst[:, C_POS:C_POS + NB], S(blk)[:, n:n + 1], w_flat[:, n:n + 1],
                   ALU.is_equal, ALU.mult).then_inc(hot_ready, 1)
            hidden(1, 1)
            dve.wait_ge(hot_used, TOPK * LT)
            then(ts(ids[:, :], bank(7, NB), -1.0, cst[:, C_SPARE:C_SPARE + 1], ALU.mult, ALU.add))
            V.tensor_copy(wts[:, :], bank(7, NB, NB)).then_inc(ids_ready, 1)
            start_sums(1)

            def keep_rows():
                for k in range(4):
                    ins = nc.vector.tensor_scalar(xeT[:, k, :], bank(2, P, k * P), mod2[:, 1, k:k + 1], mod2[:, 0, k:k + 1],
                                                  ALU.mult, ALU.add)
                ins.then_inc(xT_dve, 1)

            total = dve.value_load(nb_tab[0:1, 2 * E:2 * E + 1], min_val=1, max_val=BLOCKS)
            dve.wait_ge(ids_ready, 1)
            dve.wait_ge(xT_done, 1)
            keep_rows()
            V.memset(w_now[:, :], 0.0).then_inc(y_ready, 1)
            with dve.Fori(0, total) as b:
                dve.wait_ge(y_ready, b + 1)
                V.tensor_copy(w_now[:, :], wts[:, bass.ds(b, 1)]).then_inc(w_ready, 1)
                for f in range(2):
                    dve.wait_ge(esil, b * 2 + f + 1)
                    tt(hmE[:, f, :], bank(f, P, P), silE[:, f, :], ALU.mult).then_inc(ehm, 1)
                dve.wait_ge(xT_done, b + 2)
                keep_rows()
                dve.wait_ge(edown, b + 1)
                dve.wait_ge(scattered, b * 16 + 16)
                dve.wait_ge(w_ready, b + 1)
                for h in range(2):
                    ins = stt(ye[:, HALVES[h]], bank(4 + h), w_now[:, 0:1], gates[:, 1, HALVES[h]], ALU.mult, ALU.mult)
                ins.then_inc(y_ready, 1)

            dve.wait_ge(ln2_in, 32)
            for i in range(LT):
                z = z1[:, i, :]
                dve.wait_ge(acc_in[i], 16)
                for s in range(2):
                    then(nc.vector.bn_stats(stats[:, s, :], z[:, s * 512:(s + 1) * 512]))
                nc.vector.bn_aggr(mv[:, i, :], stats[:, :, :].rearrange("p a b -> p (a b)")).then_inc(var5, 1)
                dve.wait_ge(var5, i + 1)
                if i >= 1:
                    finish_row(dve, then, i - 1)
            finish_row(dve, then, LT - 1)

        def finish_row(dve, then, i):
            z = z1[:, i, :]
            dve.wait_ge(rstd5, i + 1)
            then(nc.vector.tensor_scalar(z, z, mv[:, i, 0:1], rstd[:, i:i + 1], ALU.subtract, ALU.mult))
            nc.vector.tensor_tensor(z, z, ln2_rows[:, 0, :], ALU.mult).then_inc(norm5, 1)

        def stage3_gpsimd(pool, then):
            def inv_root1(i):
                then(nc.gpsimd.tensor_scalar(rstd[:, i:i + 1], mv[:, i, 1:2], 1.0, EPS, ALU.mult, ALU.add))
                return nc.gpsimd.tensor_tensor(rstd[:, i:i + 1], rstd[:, i:i + 1], mhalf[:, 0:1], ALU.pow)

            then(nc.gpsimd.memset(ones_t[:, :], 1.0))
            pool.wait_ge(ln1_in, 32)
            for i in range(LT):
                z = z1[:, i, :]
                pool.wait_ge(var3, 2 * i + 1)
                inv_root1(i).then_inc(rstd3, 1)
                pool.wait_ge(norm3, i + 1)
                then(nc.gpsimd.tensor_tensor(z, z, ln_rows[:, 0, :], ALU.mult))
                nc.gpsimd.tensor_tensor(z, z, ln_rows[:, 1, :], ALU.add).then_inc(gain3, 1)
                pool.wait_ge(var3, 2 * i + 2)
                inv_root1(i).then_inc(rstd3, 1)
            nc.gpsimd.tensor_copy(exact[:, 0:P], cst[:, C_TRI:C_TRI + P])
            nc.gpsimd.tensor_copy(exact[:, P:2 * P], ones_t[:, :]).then_inc(exact_ready, 1)
            pool.wait_ge(fills_in, 32)

            def carry(n):
                nc.gpsimd.tensor_tensor(mark[:, n:n + 1], ones_t[:, 0:1], ones_t[:, 0:1], ALU.mult)

            def fetch():
                nc.gpsimd.indirect_dma_start(
                    out=xe, out_offset=None, in_=zn_dram,
                    in_offset=bass.IndirectOffsetOnAxis(ap=id_in[:, 0:1], axis=0)).then_inc(gathered, 16)

            pool.wait_ge(ids_ready, 1)
            pool.wait_ge(zn_out[0], 64)
            pool.wait_ge(zn_out[1], 64)
            nc.gpsimd.dma_start(acc_dram[SEQ:SEQ + P, :], zero_rows).then_inc(scattered, 16)
            total = pool.value_load(nb_tab[0:1, 2 * E:2 * E + 1], min_val=1, max_val=BLOCKS)
            nc.gpsimd.tensor_copy(id_in[:, :], ids[:, 0:1]).then_inc(id_step, 1)
            pool.wait_ge(id_step, 1)
            fetch()
            pool.wait_ge(xT_done, 1)
            pool.wait_ge(gathered, 16)
            nc.gpsimd.tensor_copy(id_in[:, :], ids[:, 1:2]).then_inc(id_step, 1)
            pool.wait_ge(id_step, 2)
            fetch()
            pool.wait_ge(acc_out, 16 * LT)
            with pool.Fori(0, total) as b:
                pool.wait_ge(xT_done, b + 2)
                pool.wait_ge(gathered, b * 16 + 32)
                nc.gpsimd.tensor_copy(id_in[:, :], ids[:, bass.ds(b + 2, 1)]).then_inc(id_step, 1)
                pool.wait_ge(id_step, b * 2 + 3)
                carry(0)
                fetch()
                pool.wait_ge(scattered, b * 16 + 16)
                nc.gpsimd.tensor_copy(id_out[:, :], ids[:, bass.ds(b, 1)]).then_inc(id_step, 1)
                pool.wait_ge(id_step, b * 2 + 4)
                pool.wait_ge(y_ready, b + 2)
                carry(1)
                nc.gpsimd.indirect_dma_start(
                    out=acc_dram, out_offset=bass.IndirectOffsetOnAxis(ap=id_out[:, 0:1], axis=0),
                    in_=ye, in_offset=None, compute_op=ALU.add).then_inc(scattered, 16)
            pool.wait_ge(gathered, total * 16 + 32)
            carry(0)
            pool.wait_ge(ln2_in, 32)
            for i in range(LT):
                pool.wait_ge(var5, i + 1)
                inv_root1(i).then_inc(rstd5, 1)
                if i >= 1:
                    pool.wait_ge(norm5, i)
                    z = z1[:, i - 1, :]
                    nc.gpsimd.tensor_tensor(z, z, ln2_rows[:, 1, :], ALU.add).then_inc(final_ready, 1)
            pool.wait_ge(norm5, LT)
            z = z1[:, LT - 1, :]
            nc.gpsimd.tensor_tensor(z, z, ln2_rows[:, 1, :], ALU.add).then_inc(final_ready, 1)

        @block.sync
        def _(sp):
            sp.dma_start(cst[:, :], const).then_inc(consts_in, 16)
            for at, n, src in ((R_C, 8, c[0]), (R_CC, 8, c_ctx), (R_MOD1, 16, ada_b[0:2 * D]),
                               (R_MOD2, 16, ada_b[3 * D:5 * D]), (R_PSC, 2, pool_scale), (R_CB, 2, conv_b),
                               (R_LG, 2, conv_ln_g), (R_LB, 2, conv_ln_b), (R_QG, 2, q_norm_g), (R_KVG, 1, kv_norm_g)):
                sp.dma_start(rows[at:at + n, :], RV(src, n)).then_inc(rows_in, 16)
            sp.dma_start(rows[R_DW:R_DW + 2 * TAPS, :],
                         conv_dw.rearrange("t (h q) -> (t h) q", q=P)).then_inc(rows_in, 16)
            sp.dma_start(xz[:, 0:CT, :], ctx[0].rearrange("(t p) d -> p t d", p=P)).then_inc(x_in[0], 16)
            for g in (1, 2):
                a = (g - 1) * 4
                sp.dma_start(xz[:, CT + a:CT + a + 4, :],
                             x[0, a * P:(a + 4) * P].rearrange("(t p) d -> p t d", p=P)).then_inc(x_in[g], 16)

            def ada_piece(n):
                at = n if n < 8 else n % 2
                if n in (8, 9):
                    sp.wait_ge(ada_used, n - 7)
                if n >= 10:
                    sp.wait_ge(ada_summed, n - 9)
                a = ada_col(ADA_PIECES[n])
                sp.dma_start(ada[at], ada_w[:, a:a + 256].rearrange("(k p) f -> p k f", p=P))\
                    .then_inc(ada_in[at], 16)

            for n in range(8):
                ada_piece(n)
            sp.dma_start(win[:, :, 0:QKV], w_in[:, 0:QKV].rearrange("(k p) f -> p k f", p=P)).then_inc(win_in, 16)
            for m in range(2):
                a = 2 * D if m == 0 else 5 * D
                sp.dma_start(gates[:, m, :], ada_b[a:a + D].partition_broadcast(P)).then_inc(gates_in, 16)
            sp.dma_start(win[:, :, QKV:IN_COLS], w_in[:, QKV:IN_COLS].rearrange("(k p) f -> p k f", p=P)).then_inc(win2_in, 16)
            sp.dma_start(wuq, w_uq.rearrange("(k p) f -> p k f", p=P)).then_inc(wq_in, 16)
            sp.dma_start(wukv, w_ukv).then_inc(wq_in, 16)
            sp.wait_ge(zeros_ready, 1)
            for g in range(4):
                o = PG * (g % 2)
                sp.dma_start(bdiag[o:o + PG, g // 2, o:o + PG], pool_w[g]).then_inc(diag_in, 16)
            for n in range(8, 24):
                ada_piece(n)
            sp.wait_ge(job_done, ring.of[("V", 0)][0])
            sp.dma_start(wout, w_out.rearrange("(k p) f -> p k f", p=P)).then_inc(wout_in, 16)
            stage3_loads(sp)

        @block.tensor
        def _(pe):
            n_ring = [0]

            def ring_bank(name):
                n = ring.of[name][0]
                assert n == n_ring[0], name
                n_ring[0] += 1
                if n >= 4:
                    job_emptied(pe, ring.jobs[n - 4][0])
                return bank(n % 4)

            pe.wait_ge(consts_in, 16)
            pe.wait_ge(rows_in, 16 * 11)
            o = ring_bank(("rows",))
            nc.tensor.transpose(o[:, 0:N_ROWS], rows[0:N_ROWS, :], ident[0:N_ROWS, 0:N_ROWS]).then_inc(job_done, 1)

            pe.wait_ge(silu_ready, 1)
            pe.wait_ge(zeros_ready, 1)

            def mod_cols(r):
                pe.wait_ge(mod_rows, r + 1)
                for j in range(4 * r, 4 * r + 4):
                    mm = nc.tensor.transpose(bank(4, 2, 2 * j), mrow[0:2, j * P:(j + 1) * P], ident[0:2, 0:2])
                return mm

            for q in range(8):
                r = q // 2
                pe.wait_ge(ada_in[q], 16)
                if q == 6:
                    pe.wait_ge(mod_rows, 1)
                for k in range(KD):
                    mm = nc.tensor.matmul(bank(5 + r % 3, 256, 256 * (q % 2))[0:2, :], sc[:, k:16:8], ada[q][:, k, :],
                                          start=k == 0, stop=k == KD - 1)
                mm.then_inc(ada_used, 1)
                if q in (3, 5):
                    mod_cols(r - 1)
            mod_cols(2)
            mod_cols(3).then_inc(mod_sum, 1)

            def second_cols(q):
                n = 8 + q
                pe.wait_ge(ada_summed, n + 1)
                if q == 0:
                    pe.wait_ge(mod_ready, 1)
                for s in range(2):
                    mm = nc.tensor.matmul(bank(4, 2, 2 * (2 * q + s)), ada_acc[:, n % 3, P * s:P * (s + 1)], ada_ones[:, 0:2],
                                          start=True, stop=True)
                mm.then_inc(ada_used, 1)
            for g, (a, b) in enumerate(groups):
                pe.wait_ge(z_ready, b)
                for k in range(KD):
                    o = ring_bank(("hT", g, k))
                    for t in range(a, b):
                        mm = nc.tensor.transpose(o[:, (t - a) * P:(t - a + 1) * P], xz[:, t, k * P:(k + 1) * P], ident)
                    mm.then_inc(job_done, 1)
            pe.wait_ge(win_in, 16)
            for i in range(NT):
                if i in (0, 2, 6):
                    g = (0, 2, 6).index(i)
                    job_emptied(pe, ("hT", g, KD - 1))
                    job_emptied(pe, ("hT", g, KD - 2))
                o = ring_bank(("qkv", i))
                lo = QL if i < CT else 0
                for k in range(KD):
                    mm = nc.tensor.matmul(o[:, lo:QKV], hT[:, k, i * P:(i + 1) * P], win[:, k, lo:QKV],
                                          start=k == 0, stop=k == KD - 1)
                mm.then_inc(job_done, 1)
            pe.wait_ge(win2_in, 16)
            cols = {"pool": QKV, "ca": QKV + CW, "cg": QKV + 2 * CW}
            n_mixed = 0
            for name, _ in ring.jobs:
                if name[0] in cols:
                    kind, j, n = name
                    o = ring_bank(name)
                    a = cols[kind] + P * j
                    for k in range(KD):
                        mm = nc.tensor.matmul(o, win[:, k, a:a + P], hT[:, k, CTX + 512 * n:CTX + 512 * (n + 1)],
                                              start=k == 0, stop=k == KD - 1)
                    mm.then_inc(job_done, 1)
                    if 8 <= n_mixed < 11:
                        second_cols(2 * (n_mixed - 8))
                        second_cols(2 * (n_mixed - 8) + 1)
                    n_mixed += 1
                elif name[0] == "gate":
                    o = ring_bank(name)
                    n = 4 * name[1] + name[2]
                    pe.wait_ge(ada_summed, n + 1)
                    nc.tensor.matmul(o[:, 0:256], ada_ones, ada_acc[:, n % 3, :], start=True, stop=True).then_inc(job_done, 1)
            pe.wait_ge(lat_ready, NT)
            for c_ in range(2):
                for n in range(2):
                    o = ring_bank(("qcT", c_, n))
                    for t in range(4):
                        mm = nc.tensor.transpose(o[:, t * P:(t + 1) * P], qkv[:, CT + 4 * n + t, c_ * P:(c_ + 1) * P], ident)
                    mm.then_inc(job_done, 1)
            for kind, lo, m in (("kvT", QL, P), ("krT", QKV - HD, HD)):
                if kind == "krT":
                    pe.wait_ge(kr_ready, 1)
                for g, (a, b) in enumerate(groups):
                    o = ring_bank((kind, g))
                    for t in range(a, b):
                        mm = nc.tensor.transpose(o[0:m, (t - a) * P:(t - a + 1) * P], qkv[:, t, lo:lo + m], ident)
                    mm.then_inc(job_done, 1)
            second_cols(6)
            second_cols(7)
            pe.wait_ge(wq_in, 32)
            job_emptied(pe, ("kvT", 2))
            wv = wukv.rearrange("p (h e) -> p h e", h=HEADS)[:, :, NOPE:NOPE + VD]
            for i in range(NT):
                o = ring_bank(("V", i))
                nc.tensor.matmul(o, kvT[:, i * P:(i + 1) * P], wv, start=True, stop=True).then_inc(job_done, 1)

            n_slot = {"a": 0, "b": 0}

            def slot(name, b):
                assert slot_no[name] == (b, n_slot[b] + 1), name
                if n_slot[b]:
                    pe.wait_ge(cleared[b], n_slot[b])
                n_slot[b] += 1
                o = bank(SLOT_BANK[b])
                kind = name[0]
                if kind == "P":
                    _, i, part = name
                    if part == 0:
                        pe.wait_ge(probs_ready, i + 1)
                    for t in range(4 * part, min(4 * part + 4, NT)):
                        mm = nc.tensor.transpose(o[:, (t - 4 * part) * P:(t - 4 * part + 1) * P],
                                                 probs[:, i % 2, t * P:(t + 1) * P], ident)
                elif kind == "q":
                    _, h, n = name
                    for t in range(4):
                        for c_ in range(2):
                            mm = nc.tensor.matmul(o[:, t * HD:(t + 1) * HD], qcT[:, c_, (4 * n + t) * P:(4 * n + t + 1) * P],
                                                  wuq[:, c_, h * HD:(h + 1) * HD], start=c_ == 0, stop=c_ == 1)
                elif kind in ("qraw", "qrot"):
                    _, h, n = name
                    src = qraw[:, h % 2] if kind == "qraw" else qrot
                    if kind == "qraw":
                        slot_cleared(pe, ("q", h, n))
                    else:
                        pe.wait_ge(rope_ready, h + 1)
                    for t in range(4):
                        mm = nc.tensor.transpose(o[0:HD, t * P:(t + 1) * P], src[:, 4 * n + t, :], ident)
                elif kind == "kn":
                    _, h, n = name
                    w = min(512, KEYS - 512 * n)
                    mm = nc.tensor.matmul(o[0:NOPE, 0:w], wukv[:, h * P:h * P + NOPE], kvT[:, 512 * n:512 * n + w],
                                          start=True, stop=True)
                elif kind == "O":
                    _, p, n = name
                    pe.wait_ge(O_kept, 2 * LT * (p + 1))
                    for t in range(4):
                        mm = nc.tensor.transpose(o[:, t * P:(t + 1) * P], Opair[p % 2][:, 4 * n + t, :], ident)
                elif kind == "pool":
                    _, j, n = name
                    pe.wait_ge(pdif_ready, 2)
                    pe.wait_ge(diag_in, 64)
                    mm = nc.tensor.matmul(o, bdiag[:, j, :], pdif[:, j, 512 * n:512 * (n + 1)], start=True, stop=True)
                elif kind == "y":
                    _, s = name
                    pe.wait_ge(conv_ready, 2 * TAPS)
                    for t in range(2):
                        for j in range(2):
                            mm = nc.tensor.transpose(o[:, (2 * t + j) * P:(2 * t + j + 1) * P],
                                                     yconv[:, j, (2 * s + t) * P:(2 * s + t + 1) * P], ident)
                elif kind == "yT":
                    _, j, n = name
                    pe.wait_ge(ytok_ready, LT)
                    for t in range(4):
                        mm = nc.tensor.transpose(o[:, t * P:(t + 1) * P], ytok[:, 4 * n + t, j * P:(j + 1) * P], ident)
                mm.then_inc(filled[b], 1)

            job_emptied(pe, ("qcT", 1, 0))
            job_emptied(pe, ("qcT", 1, 1))
            for name, b in prep_slots(0):
                slot(name, b)
            pe.wait_ge(emptied["act"], ring.n["act"])
            pe.wait_ge(emptied["dve"], ring.n["dve"])

            def scores(i):
                h, qt = i // LT, i % LT
                if qt == 0:
                    for name, _ in prep_slots(h):
                        if name[0] != "q":
                            slot_cleared(pe, name)
                if i >= 2:
                    pe.wait_ge(probs_ready, i - 1)
                qs = slice(qt * P, (qt + 1) * P)
                lat = 0 if i % 2 == 0 else 3
                for n in range(2):
                    nc.tensor.matmul(bank(lat + n), QT[0:HD, h % 2, 1, qs], KT[0:HD, h % 2, CTX + 512 * n:CTX + 512 * (n + 1)],
                                     start=True, stop=True)
                if i >= 1:
                    pe.wait_ge(probs_ready, i)
                nc.tensor.matmul(bank(2, 256, 256 * (i % 2)), QT[0:HD, h % 2, 0, qs], KT[0:HD, h % 2, 0:CTX],
                                 start=True, stop=True).then_inc(scores_ready, 1)

            def values(i, first, last):
                h = i // LT
                if first == 0:
                    for part in range(3):
                        slot_cleared(pe, ("P", i, part))
                    if i >= 1:
                        pe.wait_ge(O_kept, i)
                for t in range(first, last):
                    key = (t + CT) % NT if i % 2 == 0 else t
                    mm = nc.tensor.matmul(bank(7, VD), probsT[:, i % 2, t, :], V[:, key, h * VD:(h + 1) * VD],
                                          start=t == 0, stop=t == NT - 1)
                if last == NT:
                    mm.then_inc(O_ready, 1)

            for i, named in enumerate(slots_at):
                if i < UNITS:
                    scores(i)
                mine = [s for s in named if s[0][0] == "P"]
                for s in mine[:2]:
                    slot(*s)
                if 2 <= i < UNITS + 2:
                    values(i - 2, 0, 6)
                for s in mine[2:]:
                    slot(*s)
                if 2 <= i < UNITS + 2:
                    values(i - 2, 6, NT)
                for s in named:
                    if s[0][0] != "P":
                        slot(*s)
            stage3_tensor(pe)

        @block.scalar
        def _(act):
            job_emptied(act, ("rows",))
            nc.scalar.activation(sc[:, :], col[:, 0:16], ACT.Silu).then_inc(silu_ready, 1)
            for r in range(4):
                act.wait_ge(ada_used, 2 * r + 2)
                nc.scalar.copy(mrow[0:2, 512 * r:512 * (r + 1)], bank(5 + r % 3)[0:2, :]).then_inc(mod_rows, 1)
            first_hT = True
            for name, e in ring.jobs:
                if e != "act":
                    continue
                n = ring.of[name][0]
                b = bank(n % 4)
                kind = name[0]
                if kind == "hT" and first_hT:
                    act.wait_ge(mod_ready, 1)
                    first_hT = False
                act.wait_ge(job_done, n + 1)
                if kind == "hT":
                    _, g, k = name
                    a, z = groups[g]
                    w = 0 if g else 1
                    ins = nc.scalar.activation(hT[:, k, a * P:z * P], b[:, 0:(z - a) * P], ACT.Identity,
                                               bias=mod1[:, 0, k, w:w + 1], scale=mod1[:, 1, k, w:w + 1])
                elif kind == "qkv":
                    i = name[1]
                    lo = QL if i < CT else 0
                    ins = nc.scalar.copy(qkv[:, i, lo:QKV], b[:, lo:QKV])
                elif kind == "pool":
                    _, j, m = name
                    act.wait_ge(pads_ready, 1)
                    ins = nc.scalar.copy(upool[:, j, PPAD + 512 * m:PPAD + 512 * (m + 1)], b)
                elif kind == "cg":
                    _, j, m = name
                    at = 2 * j + m
                    if at >= 2:
                        job_emptied(act, ("ca", (at - 2) // 2, (at - 2) % 2))
                    ins = nc.scalar.activation(sig[:, at % 2, :], b, ACT.Sigmoid)
                elif kind == "qcT":
                    _, c_, m = name
                    ins = nc.scalar.activation(qcT[:, c_, 512 * m:512 * (m + 1)], b, ACT.Copy, scale=col[:, R_QG + c_:R_QG + c_ + 1])
                elif kind == "kvT":
                    a, z = groups[name[1]]
                    ins = nc.scalar.activation(kvT[:, a * P:z * P], b[:, 0:(z - a) * P], ACT.Copy, scale=col[:, R_KVG:R_KVG + 1])
                elif kind == "V":
                    ins = nc.scalar.copy(V[:, name[1], :], b)
                ins.then_inc(emptied["act"], 1)
                if name == ("qkv", NT - 2):
                    count = 0
                    act.wait_ge(zeros_ready, 1)
                    for i in range(NT):
                        job_emptied(act, ("qkv", i))
                        for m, lo, w in ((0, 0, QL), (1, QL, KVL)):
                            if m == 0 and i < CT:
                                continue
                            if count:
                                act.wait_ge(ssq_ready, count)
                            nc.scalar.activation(junk[:, 0:w], qkv[:, i, lo:lo + w], ACT.Square,
                                                 accum_out=ssq[:, i, m:m + 1]).then_inc(ssq_ready, 1)
                            count += 1

            def evac(name, b):
                n = slot_no[name][1]
                act.wait_ge(filled[b], n)
                o = bank(SLOT_BANK[b])
                kind = name[0]
                if kind == "P":
                    _, i, part = name
                    if i >= 2 and part == 0:
                        act.wait_ge(O_ready, i - 1)
                    t0 = 4 * part
                    t1 = min(t0 + 4, NT)
                    ins = nc.scalar.copy(probsT[:, i % 2, t0:t1, :].rearrange("p t q -> p (t q)"), o[:, 0:(t1 - t0) * P])
                elif kind == "q":
                    _, h, m = name
                    if h >= 2:
                        act.wait_ge(rope_ready, h - 1)
                    ins = nc.scalar.copy(qraw[:, h % 2, 4 * m:4 * m + 4, :].rearrange("p t q -> p (t q)"), o[:, 0:4 * HD])
                elif kind in ("qraw", "qrot"):
                    _, h, m = name
                    ins = nc.scalar.copy(QT[0:HD, h % 2, int(kind == "qrot"), 512 * m:512 * (m + 1)], o[0:HD, :])
                elif kind == "kn":
                    _, h, m = name
                    w = min(512, KEYS - 512 * m)
                    ins = nc.scalar.copy(KT[0:NOPE, h % 2, 512 * m:512 * m + w], o[0:NOPE, 0:w])
                elif kind == "O":
                    _, p, m = name
                    if p == 0 and m == 0:
                        act.wait_ge(pdif_ready, 2)
                    ins = nc.scalar.copy(mixT[:, p, 512 * m:512 * (m + 1)], o)
                elif kind == "yT":
                    _, j, m = name
                    ins = nc.scalar.activation(yconv[:, j, 512 * m:512 * (m + 1)], o, ACT.Identity,
                                               bias=col[:, R_LB + j:R_LB + j + 1], scale=col[:, R_LG + j:R_LG + j + 1])
                ins.then_inc(cleared[b], 1)

            for name, b in prep_slots(0):
                if b == "a":
                    evac(name, b)

            def exp(i):
                act.wait_ge(nmax_ready, i + 1)
                if i >= 2:
                    b, n = slot_no[("P", i - 2, 2)]
                    act.wait_ge(filled[b], n)
                    b, n = slot_no[("P", i - 2, 1)]
                    act.wait_ge(filled[b], n)
                if i >= 4:
                    act.wait_ge(O_kept, i - 3)
                at = KEYS * (i % 2)
                nc.scalar.activation(probs[:, i % 2, :], psum[:, at:at + KEYS], ACT.Exp, bias=nmax[:, 2 + i % 2:3 + i % 2],
                                     scale=SCALE, accum_out=rsum[:, i % 4:i % 4 + 1]).then_inc(probs_ready, 1)

            for i, named in enumerate(slots_at):
                mine = [s for s in named if s[1] == "a"]
                for s in mine:
                    if s[0][0] == "P" and s[0][2] == 0:
                        evac(*s)
                if i < UNITS:
                    exp(i)
                for s in mine:
                    if not (s[0][0] == "P" and s[0][2] == 0):
                        evac(*s)
            stage3_scalar(act)

        @block.vector
        def _(dve):
            steps = [0]

            def then(ins):
                chain(dve, dve_step, steps, ins)

            dve.wait_ge(consts_in, 16)
            dve.wait_ge(job_done, 1)
            nc.vector.tensor_copy(col[:, :], bank(0, N_ROWS)).then_inc(emptied["dve"], 1)

            n_z = 0
            for g, (a, b) in enumerate(groups):
                dve.wait_ge(x_in[g], 16)
                for t in range(a, b):
                    for s in range(2):
                        then(nc.vector.bn_stats(stats[:, s, :], xz[:, t, s * 512:(s + 1) * 512]))
                    nc.vector.bn_aggr(mv[:, t, :], stats[:, :, :].rearrange("p a b -> p (a b)")).then_inc(var_ready, 1)
                    dve.wait_ge(var_ready, t + 1)
            for g, (a, b) in enumerate(groups):
                dve.wait_ge(rstd_ready, g + 1)
                for t in range(a, b):
                    nc.vector.tensor_scalar(xz[:, t, :], xz[:, t, :], mv[:, t, 0:1], rstd[:, t:t + 1],
                                            ALU.subtract, ALU.mult).then_inc(z_ready, 1)
            dve.wait_ge(silu_ready, 1)
            dve.wait_ge(mod_sum, 1)
            for w in range(2):
                then(nc.vector.tensor_tensor(mod1[:, :, :, w].rearrange("p a k -> p (a k)"),
                                             bank(4, 32).rearrange("p (k w) -> p k w", w=2)[:, :, w],
                                             col[:, R_MOD1:R_MOD1 + 16], ALU.add))
            nc.vector.tensor_scalar(mod1[:, 1, :, :], mod1[:, 1, :, :], 1.0, None, ALU.add).then_inc(mod_ready, 1)
            dve.wait_ge(mod_ready, 1)

            taps, summed = [0], [0]

            def sum_piece():
                n = summed[0]
                summed[0] += 1
                dve.wait_ge(ada_in[n % 2], 16 * (n // 2 + 2))
                if n >= 11:
                    dve.wait_ge(ada_used, n - 2)
                elif n >= 3:
                    dve.wait_ge(job_done, ring.of[("gate", (n - 3) // 4, (n - 3) % 4)][0] + 1)
                w, acc = ada[n % 2], ada_acc[:, n % 3, :]
                for k in range(KD):
                    if k == 0:
                        ins = nc.vector.tensor_scalar(acc, w[:, k, :], sc[:, k:k + 1], None, ALU.mult)
                    else:
                        ins = nc.vector.scalar_tensor_tensor(acc, w[:, k, :], sc[:, k:k + 1], acc, ALU.mult, ALU.add)
                    if k < KD - 1:
                        then(ins)
                ins.then_inc(ada_summed, 1)

            def tap():
                n = taps[0]
                if n >= 2 * TAPS:
                    return
                taps[0] += 1
                t, j = n // 2, n % 2
                w = col[:, R_DW + n:R_DW + n + 1]
                u = uconv[:, j, t:t + SEQ]
                if t == 0:
                    ins = nc.vector.tensor_scalar(yconv[:, j, :], u, w, col[:, R_CB + j:R_CB + j + 1], ALU.mult, ALU.add)
                else:
                    dve.wait_ge(conv_ready, n - 1)
                    ins = nc.vector.scalar_tensor_tensor(yconv[:, j, :], u, w, yconv[:, j, :], ALU.mult, ALU.add)
                ins.then_inc(conv_ready, 1)

            for name, e in ring.jobs:
                if e != "dve" or name[0] == "rows":
                    continue
                n = ring.of[name][0]
                b = bank(n % 4)
                kind = name[0]
                dve.wait_ge(job_done, n + 1)
                if kind == "hT":
                    _, g, k = name
                    a, z = groups[g]
                    w = 0 if g else 1
                    ins = nc.vector.tensor_scalar(hT[:, k, a * P:z * P], b[:, 0:(z - a) * P], mod1[:, 1, k, w:w + 1],
                                                  mod1[:, 0, k, w:w + 1], ALU.mult, ALU.add)
                elif kind == "qkv":
                    i = name[1]
                    lo = QL if i < CT else 0
                    ins = nc.vector.tensor_copy(qkv[:, i, lo:QKV], b[:, lo:QKV])
                elif kind == "ca":
                    _, j, m = name
                    job_emptied(dve, ("cg", j, m))
                    ins = nc.vector.tensor_tensor(uconv[:, j, CPAD + 512 * m:CPAD + 512 * (m + 1)], b,
                                                  sig[:, (2 * j + m) % 2, :], ALU.mult)
                elif kind == "gate":
                    _, m, q = name
                    if m == 0 and q == 0:
                        dve.wait_ge(gates_in, 32)
                    g_ = gates[:, m, 256 * q:256 * (q + 1)]
                    ins = nc.vector.tensor_tensor(g_, b[:, 0:256], g_, ALU.add)
                elif kind == "qcT":
                    _, c_, m = name
                    ins = nc.vector.tensor_scalar(qcT[:, c_, 512 * m:512 * (m + 1)], b, col[:, R_QG + c_:R_QG + c_ + 1], None, ALU.mult)
                elif kind == "krT":
                    g = name[1]
                    a, z = groups[g]
                    ins = nc.vector.tensor_copy(KT[NOPE:HD, 0, a * P:z * P], b[NOPE:HD, 0:(z - a) * P])
                    nc.vector.tensor_copy(KT[NOPE:HD, 1, a * P:z * P], b[NOPE:HD, 0:(z - a) * P]).then_inc(emptied["dve"], 1)
                    ins = None
                elif kind == "V":
                    ins = nc.vector.tensor_copy(V[:, name[1], :], b)
                if ins is not None:
                    ins.then_inc(emptied["dve"], 1)
                if name in (("qkv", 5), ("qkv", 7), ("qkv", 9), ("ca", 1, 1)) or kind in ("gate", "ca"):
                    sum_piece()
                if name == ("ca", 1, 1):
                    sum_piece()
                if name == ("gate", 0, 1):
                    dve.wait_ge(rq_ready, 1)
                    for i in range(NT):
                        if i >= CT:
                            then(nc.vector.tensor_scalar(qkv[:, i, 0:QL], qkv[:, i, 0:QL], rq[:, i, 0:1], None, ALU.mult))
                        nc.vector.tensor_scalar(qkv[:, i, QL:QL + KVL], qkv[:, i, QL:QL + KVL], rq[:, i, 1:2], None,
                                                ALU.mult).then_inc(lat_ready, 1)
                if name == ("krT", 2):
                    dve.wait_ge(ada_used, 16)
                    then(nc.vector.tensor_tensor(mod2[:, :, :].rearrange("p a k -> p (a k)"),
                                                 bank(4, 32).rearrange("p (k w) -> p k w", w=2)[:, :, 0],
                                                 col[:, R_MOD2:R_MOD2 + 16], ALU.add))
                    nc.vector.tensor_scalar(mod2[:, 1, :], mod2[:, 1, :], 1.0, None, ALU.add).then_inc(mod_ready, 1)
                    job_emptied(dve, ("ca", 1, 1))
                    dve.wait_ge(zeros_ready, 1)

            def evac(name, b):
                n = slot_no[name][1]
                dve.wait_ge(filled[b], n)
                o = bank(SLOT_BANK[b])
                kind = name[0]
                if kind == "P":
                    _, i, part = name
                    if i >= 2:
                        dve.wait_ge(O_ready, i - 1)
                    t0 = 4 * part
                    ins = nc.vector.tensor_copy(probsT[:, i % 2, t0:t0 + 4, :].rearrange("p t q -> p (t q)"), o)
                elif kind == "q":
                    _, h, m = name
                    if h >= 2:
                        dve.wait_ge(rope_ready, h - 1)
                    ins = nc.vector.tensor_copy(qraw[:, h % 2, 4 * m:4 * m + 4, :].rearrange("p t q -> p (t q)"), o[:, 0:4 * HD])
                elif kind in ("qraw", "qrot"):
                    _, h, m = name
                    ins = nc.vector.tensor_copy(QT[0:HD, h % 2, int(kind == "qrot"), 512 * m:512 * (m + 1)], o[0:HD, :])
                elif kind == "kn":
                    _, h, m = name
                    w = min(512, KEYS - 512 * m)
                    ins = nc.vector.tensor_copy(KT[0:NOPE, h % 2, 512 * m:512 * m + w], o[0:NOPE, 0:w])
                elif kind == "O":
                    _, p, m = name
                    if p == 0:
                        dve.wait_ge(pdif_ready, 2)
                    ins = nc.vector.tensor_copy(mixT[:, p, 512 * m:512 * (m + 1)], o)
                elif kind == "pool":
                    _, j, m = name
                    ins = nc.vector.tensor_scalar(mixT[:, 4 + j, 512 * m:512 * (m + 1)], o, col[:, R_PSC + j:R_PSC + j + 1], None, ALU.mult)
                elif kind == "y":
                    s = name[1]
                    ins = nc.vector.tensor_copy(ytok[:, 2 * s:2 * s + 2, :].rearrange("p t c -> p (t c)"), o)
                ins.then_inc(cleared[b], 1)

            for name, b in prep_slots(0):
                if b == "b":
                    evac(name, b)

            for _ in range(TAP_FIRST):
                tap()
            for i, named in enumerate(slots_at):
                if i < UNITS:
                    dve.wait_ge(scores_ready, i + 1)
                    at = KEYS * (i % 2)
                    m = i % 2
                    if i >= 2:
                        dve.wait_ge(probs_ready, i - 1)
                    then(nc.vector.tensor_reduce(nmax[:, m:m + 1], psum[:, at:at + KEYS], AX.X, ALU.max))
                    nc.vector.tensor_scalar(nmax[:, 2 + m:3 + m], nmax[:, m:m + 1], -SCALE, None, ALU.mult).then_inc(nmax_ready, 1)
                want = min(2 * TAPS, TAP_FIRST + (2 * TAPS - TAP_FIRST) * (i + 1) // TAP_STEP)
                for s in named:
                    if s[1] == "b" and s[0][0] == "P":
                        evac(*s)
                while taps[0] < want:
                    tap()
                if 2 <= i < UNITS + 2:
                    u = i - 2
                    h, qt, m = u // LT, u % LT, u % 2
                    dve.wait_ge(probs_ready, u + 1)
                    then(nc.vector.reciprocal(rinv[:, m:m + 1], rsum[:, u % 4:u % 4 + 1]))
                    dve.wait_ge(O_ready, u + 1)
                    if h % 2 == 0 and h >= 4 and qt == 0:
                        slot_cleared(dve, ("O", h // 2 - 2, 0))
                        slot_cleared(dve, ("O", h // 2 - 2, 1))
                    nc.vector.tensor_scalar(Opair[(h // 2) % 2][:, qt, VD * (h % 2):VD * (h % 2 + 1)], bank(7, VD),
                                            rinv[:, m:m + 1], None, ALU.mult).then_inc(O_kept, 1)
                for s in named:
                    if s[1] == "b" and s[0][0] != "P":
                        evac(*s)
                if TAP_STEP + 4 < i <= TAP_STEP + 4 + 4:
                    s = i - TAP_STEP - 5
                    slot_cleared(dve, ("y", s))
                    for t in (2 * s, 2 * s + 1):
                        then(nc.vector.bn_stats(stats[:, 0, :], ytok[:, t, :]))
                        nc.vector.bn_aggr(mv[:, t, :], stats[:, 0, :]).then_inc(var_ready, 1)
                        dve.wait_ge(var_ready, NT + t + 1)
                    if s == 3:
                        dve.wait_ge(rstd_ready, 4)
                        for t in range(LT):
                            nc.vector.tensor_scalar(ytok[:, t, :], ytok[:, t, :], mv[:, t, 0:1], rstd[:, t:t + 1],
                                                    ALU.subtract, ALU.mult).then_inc(ytok_ready, 1)
            stage3_vector(dve, then)

        @block.gpsimd
        def _(pool):
            steps = [0]

            def then(ins):
                chain(pool, pool_step, steps, ins)

            def inv_root(dst, src, scale):
                then(nc.gpsimd.tensor_scalar(dst, src, scale, EPS, ALU.mult, ALU.add))
                return nc.gpsimd.tensor_tensor(dst, dst, mhalf_like(dst), ALU.pow)

            def mhalf_like(dst):
                n = 1
                for d in dst.shape[1:]:
                    n *= d
                v = mhalf[:, 0:n]
                return v if len(dst.shape) == 2 else v.rearrange("p (a b) -> p a b", b=dst.shape[2])

            then(nc.gpsimd.memset(mhalf[:, :], -0.5))
            then(nc.gpsimd.memset(ssq[:, :, :], 1.0))
            nc.gpsimd.memset(ada_ones, 1.0)
            nc.gpsimd.memset(bdiag[:, :, :], 0.0)
            nc.gpsimd.memset(uconv[:, :, 0:CPAD], 0.0)
            nc.gpsimd.memset(uconv[:, :, CPAD + SEQ:], 0.0).then_inc(zeros_ready, 1)
            for g, (a, b) in enumerate(groups):
                pool.wait_ge(var_ready, b)
                inv_root(rstd[:, a:b], mv[:, a:b, 1], 1.0).then_inc(rstd_ready, 1)
            pool.wait_ge(job_done, ring.of[("hT", 2, KD - 1)][0] + 1)
            nc.gpsimd.memset(upool[:, :, 0:PPAD], 0.0)
            nc.gpsimd.memset(upool[:, :, PPAD + SEQ:], 0.0).then_inc(pads_ready, 1)
            pool.wait_ge(ssq_ready, NT + LT)
            then(nc.gpsimd.tensor_scalar(rq[:, :, 0], ssq[:, :, 0], 1.0 / QL, EPS, ALU.mult, ALU.add))
            then(nc.gpsimd.tensor_scalar(rq[:, :, 1], ssq[:, :, 1], 1.0 / KVL, EPS, ALU.mult, ALU.add))
            nc.gpsimd.tensor_tensor(rq[:, :, :], rq[:, :, :], mhalf_like(rq[:, :, :]), ALU.pow).then_inc(rq_ready, 1)

            cos = cst[:, C_COS:C_COS + 128].rearrange("p (t a f) -> p t a f", t=LT, a=2)
            sin = cst[:, C_SIN:C_SIN + 128].rearrange("p (t a f) -> p t a f", t=LT, a=2)

            def rotate(src, dst):
                s = src.rearrange("p t (a m f) -> p t a m f", a=2, m=2)
                d = dst.rearrange("p t (a m f) -> p t a m f", a=2, m=2)
                x1, x2 = s[:, :, :, 0, :], s[:, :, :, 1, :]
                tm = [rtmp[:, n, :].rearrange("p (t a f) -> p t a f", t=LT, a=2) for n in range(4)]
                nc.gpsimd.tensor_tensor(tm[0], x1, cos, ALU.mult)
                nc.gpsimd.tensor_tensor(tm[1], x2, sin, ALU.mult)
                nc.gpsimd.tensor_tensor(tm[2], x2, cos, ALU.mult)
                then(nc.gpsimd.tensor_tensor(tm[3], x1, sin, ALU.mult))
                nc.gpsimd.tensor_tensor(d[:, :, :, 0, :], tm[0], tm[1], ALU.subtract)
                return nc.gpsimd.tensor_tensor(d[:, :, :, 1, :], tm[2], tm[3], ALU.add)

            kr = qkv[:, CT:NT, QL + KVL:QKV]
            rotate(kr, kr).then_inc(kr_ready, 1)
            pool.wait_ge(kr_ready, 1)

            def rope_q(h):
                slot_cleared(pool, ("q", h, 0))
                slot_cleared(pool, ("q", h, 1))
                if h >= 1:
                    slot_filled(pool, ("qrot", h - 1, 0))
                    slot_filled(pool, ("qrot", h - 1, 1))
                nc.gpsimd.tensor_copy(qrot[:, :, 0:NOPE], qraw[:, h % 2, :, 0:NOPE])
                rotate(qraw[:, h % 2, :, NOPE:HD], qrot[:, :, NOPE:HD]).then_inc(rope_ready, 1)
                pool.wait_ge(rope_ready, h + 1)

            def slot_filled(eng, name):
                b, n = slot_no[name]
                eng.wait_ge(filled[b], n)

            rope_q(0)
            for j in range(2):
                for m in range(2):
                    job_emptied(pool, ("pool", j, m))
            W = SEQ + 2 * PPAD
            for j in range(2):
                src, width = upool[:, j, :], W
                for d in range(2 * j + 2):
                    step = 1 << d
                    width -= step
                    half = slice(0, P) if d <= 2 * j else slice(PG, P)
                    dst = ptmp[:, d % 2, :]
                    then(nc.gpsimd.tensor_tensor(dst[half, 0:width], src[half, 0:width], src[half, step:step + width], ALU.add))
                    w = step * 2
                    for s in range(2):
                        if POOL_W[2 * j + s] == w:
                            rows_ = slice(PG * s, PG * (s + 1))
                            o = PPAD - w // 2
                            then(nc.gpsimd.tensor_scalar(pdif[rows_, j, :], dst[rows_, o:o + SEQ],
                                                         cst[rows_, C_WINV + j:C_WINV + j + 1], None, ALU.mult))
                    src = dst
                e = cst[:, C_EDGE + 16 * j:C_EDGE + 16 * (j + 1)]
                then(nc.gpsimd.tensor_tensor(pdif[:, j, 0:PPAD], pdif[:, j, 0:PPAD], e[:, 0:PPAD], ALU.mult))
                then(nc.gpsimd.tensor_tensor(pdif[:, j, SEQ - PPAD:SEQ], pdif[:, j, SEQ - PPAD:SEQ], e[:, PPAD:16], ALU.mult))
                nc.gpsimd.tensor_tensor(pdif[:, j, :], pdif[:, j, :], upool[:, j, PPAD:PPAD + SEQ], ALU.subtract)\
                    .then_inc(pdif_ready, 1)
            for h in range(1, HEADS):
                rope_q(h)
                if h == (TAP_STEP + 10) // LT:
                    pool.wait_ge(var_ready, NT + LT)
                    inv_root(rstd[:, 0:LT], mv[:, 0:LT, 1], 1.0).then_inc(rstd_ready, 1)
            stage3_gpsimd(pool, then)


NAMES = ("x", "c", "ctx", "c_ctx", "ada_w", "ada_b", "w_in", "q_norm_g", "w_uq", "kv_norm_g", "w_ukv", "pool_w",
         "pool_scale", "conv_dw", "conv_b", "conv_ln_g", "conv_ln_b", "conv_pw", "w_out", "ln1_g", "ln1_b",
         "router_w", "router_bias", "exp_wg", "exp_wu", "exp_wd", "sh_wg", "sh_wu", "sh_wd", "ln2_g", "ln2_b")
LAYERED = NAMES[4:]


def kernel(**inputs):
    from concourse import bacc
    from concourse.bass_utils import run_bass_kernel_spmd

    nc = bacc.Bacc("TRN2", target_bir_lowering=False, num_devices=1)
    arrays = {}
    for name in NAMES:
        a = np.asarray(inputs[name])
        arrays[name] = np.ascontiguousarray(a[0] if name in LAYERED else a)
    arrays["const"] = shape_constants()
    arrays["zero_rows"] = np.zeros((P, D), np.float32)
    args = {n: nc.dram_tensor("in_" + n, a.shape, F32, kind="ExternalInput").ap() for n, a in arrays.items()}
    out = nc.dram_tensor("out_rows", (1, SEQ, D), F32, kind="ExternalOutput").ap()
    build(nc, out=out, **args)
    r = run_bass_kernel_spmd(nc, [{"in_" + n: a for n, a in arrays.items()}], core_ids=[0])
    return r.results[0]["out_rows"]
```

```python
from contextlib import ExitStack

import numpy as np

import concourse.bass as bass
from concourse import mybir

F32 = mybir.dt.float32
F32R = mybir.dt.float32r
I32 = mybir.dt.int32
BF16 = mybir.dt.bfloat16
ALU = mybir.AluOpType
ACT = mybir.ActivationFunctionType
AX = mybir.AxisListType

P = 128
D = 1024
KD = D // P
LT, CT = 8, 2
NT = LT + CT
SEQ, CTX = LT * P, CT * P
KEYS = SEQ + CTX
GRID_W = 64
HEADS, NOPE, ROPE, VD = 8, 64, 32, 64
HD = NOPE + ROPE
QL, KVL = 256, 128
QKV = QL + KVL + ROPE
POOL_W = (2, 4, 8, 16)
PG = 64
CW = 256
TAPS = 31
CPAD = TAPS // 2
PPAD = max(POOL_W) // 2
IN_COLS = QKV + CW + 2 * CW
SCALE = float(HD) ** -0.5
ALPHA = 2.0 ** 0.25
EPS = 1e-6
E = 32
GROUPS, GE = 4, 8
TOPK = 4
FE = 256
ROUTED_SCALE = 2.5
BLOCKS = SEQ * TOPK // P + E
ACCS = 6
BIG = 1e30

R_C, R_CC, R_MOD1, R_MOD2 = 0, 8, 16, 32
R_PSC, R_CB, R_LG, R_LB, R_QG, R_KVG, R_DW = 48, 50, 52, 54, 56, 58, 59
N_ROWS = R_DW + 2 * TAPS

C_ID, C_TRI, C_WINV, C_EDGE, C_IOTA = 0, 128, 256, 258, 290
C_TOK, C_GT, C_GE, C_COS, C_SIN = 322, 330, 346, 362, 490
C_POS, C_SPARE = 618, 746
N_CONST = 747


def shape_constants():
    t = np.zeros((P, N_CONST), np.float32)
    t[:, C_ID:C_ID + P] = np.eye(P)
    t[:, C_TRI:C_TRI + P] = np.triu(np.ones((P, P)), 1)
    for j in range(2):
        for s in range(2):
            w = POOL_W[2 * j + s]
            rows = slice(PG * s, PG * (s + 1))
            t[rows, C_WINV + j] = 1.0 / w
            pos = np.concatenate([np.arange(PPAD), np.arange(SEQ - PPAD, SEQ)])
            lo, hi = w // 2, w - 1 - w // 2
            n = np.clip(pos + hi + 1, 0, SEQ) - np.clip(pos - lo, 0, SEQ)
            t[rows, C_EDGE + 16 * j:C_EDGE + 16 * (j + 1)] = w / n
    t[:, C_IOTA:C_IOTA + E] = np.arange(E) - E
    t[:, C_TOK:C_TOK + LT] = np.arange(P)[:, None] + P * np.arange(LT)
    t[:, C_POS:C_POS + P] = np.arange(P)
    t[:, C_SPARE] = SEQ + np.arange(P)
    g, j = np.meshgrid(np.arange(GROUPS), np.arange(GROUPS), indexing="ij")
    t[:, C_GT:C_GT + 16] = (j > g).reshape(-1)
    t[:, C_GE:C_GE + 16] = (j < g).reshape(-1)
    axis = ROPE // 2
    inv = (np.float32(10000.0) ** (-np.arange(0, axis, 2, dtype=np.float32) / np.float32(axis))).astype(np.float32)
    tok = np.arange(SEQ)
    row, col = (tok // GRID_W).astype(np.float32), (tok % GRID_W).astype(np.float32)
    ang = np.concatenate([row[:, None] * inv, col[:, None] * inv], axis=1)
    for at, f in ((C_COS, np.cos), (C_SIN, np.sin)):
        t[:, at:at + 128] = f(ang).astype(np.float32).reshape(LT, P, 16).transpose(1, 0, 2).reshape(P, 128)
    return t


class Ring:

    def __init__(self):
        self.jobs, self.of, self.n = [], {}, {"act": 0, "dve": 0}

    def add(self, name, engine):
        self.n[engine] += 1
        self.of[name] = (len(self.jobs), engine, self.n[engine])
        self.jobs.append((name, engine))


def stage1_jobs():
    r = Ring()
    r.add(("rows",), "dve")
    groups = [(0, 2), (2, 6), (6, 10)]
    for g in range(3):
        for k in range(KD):
            r.add(("hT", g, k), "act" if k % 2 == 0 else "dve")
    for i in range(NT):
        r.add(("qkv", i), "act" if i % 2 == 0 else "dve")
    mixed = [("pool", j, n) for j in range(2) for n in range(2)]
    mixed += [(kind, j, n) for j in range(2) for n in range(2) for kind in ("cg", "ca")]
    gates = [("gate", m, q) for m in range(2) for q in range(4)]
    for m in mixed:
        r.add(m, "dve" if m[0] == "ca" else "act")
        if gates:
            r.add(gates.pop(0), "dve")
    for c in range(2):
        for n in range(2):
            r.add(("qcT", c, n), "act" if n else "dve")
    for g in range(3):
        r.add(("kvT", g), "act")
    for g in range(3):
        r.add(("krT", g), "dve")
    for i in range(NT):
        r.add(("V", i), "act")
    return r, groups


UNITS = HEADS * LT
TAP_FIRST = 2
TAP_STEP = 45


def attention_slots():
    steps = [[] for _ in range(UNITS + 5)]
    for i in range(UNITS + 2):
        s = steps[i]
        if 1 <= i <= UNITS:
            s += [(("P", i - 1, 0), "a"), (("P", i - 1, 1), "b"), (("P", i - 1, 2), "a")]
        h, q = i // LT + 1, i % LT
        if h < HEADS and i < UNITS:
            s += sorted([(n, b) for n, b in prep_slots(h) if PREP_AT[n[0]][n[-1]] == q], key=lambda v: v[1] == "a")
    for p in range(HEADS // 2):
        at = 2 * LT * p + 2 * LT + 2
        steps[at] += [(("O", p, 0), "a"), (("O", p, 1), "b")]
    for n, at in ((0, 9), (1, 11), (2, 13), (3, 15)):
        steps[at].append((("pool", n // 2, n % 2), "b"))
    for s in range(4):
        steps[TAP_STEP + 1 + s].append((("y", s), "b"))
        steps[TAP_STEP + 11 + s].append((("yT", s // 2, s % 2), "a"))
        steps[TAP_STEP + 16 + s].append((("pw", s // 2, s % 2), "b"))
    return steps


PREP_AT = {"q": (0, 1, 2, 3), "kn": (0, 1, 3), "qraw": (2, 4), "qrot": (5, 6)}


def prep_slots(h):
    return [((kind, h, n), "a" if kind == "q" else "b")
            for kind, count in (("q", 0 if h % 2 else 4), ("kn", 3), ("qraw", 2), ("qrot", 2)) for n in range(count)]


FIRST_HEAD = {"q": (0, 0, 1, 2), "kn": (0, 2, 4), "qraw": (6, 8), "qrot": (NT, NT)}


def first_head(before):
    return [(n, b) for n, b in prep_slots(0) if FIRST_HEAD[n[0]][n[-1]] == before]


def build(nc, x, c, ctx, c_ctx, ada_w, ada_b, w_in, q_norm_g, w_uq, kv_norm_g, w_ukv, pool_w,
          pool_scale, conv_dw, conv_b, conv_ln_g, conv_ln_b, conv_pw, w_out, ln1_g, ln1_b,
          router_w, router_bias, exp_wg, exp_wu, exp_wd, sh_wg, sh_wu, sh_wd, ln2_g, ln2_b,
          const, zero_rows, out):
    with ExitStack() as stack:
        def sb(name, shape, dt=F32):
            return stack.enter_context(nc.sbuf_tensor(name, shape, dt))

        def sem(name):
            return stack.enter_context(nc.semaphore(name))

        zn_dram = nc.dram_tensor("zn_rows", [SEQ + P, D], F32, kind="Internal").ap()
        acc_dram = nc.dram_tensor("acc_rows", [SEQ + P, D], F32, kind="Internal").ap()

        LA, LB, LC, LD, LE, LF = 10240, 10240, 9472, 4864, 5184, 8192
        OA = 0
        OD = OA + LA
        OE = OD + LD
        OF = OE + LE
        OB = OF + LF
        arena = sb("arena", [P, OB])
        OC = OB + LB
        with nc.sbuf_tensor("arena_b", [P, LB + LC], F32) as arena_b:
            pass
        parts = sb("parts", [P, LB + LC], F32R)

        def part(at, n, *dims):
            v = parts[:, at - OB:at - OB + n]
            return v.rearrange("p (a b) -> p a b", a=dims[0]) if len(dims) == 1 else \
                v.rearrange("p (a b c) -> p a b c", a=dims[0], b=dims[1]) if dims else v

        def cut(at, n, *dims):
            v = arena[:, at:at + n] if at < OB else arena_b[:, at - OB:at - OB + n]
            if len(dims) == 1:
                return v.rearrange("p (a b) -> p a b", a=dims[0])
            if len(dims) == 2:
                return v.rearrange("p (a b c) -> p a b c", a=dims[0], b=dims[1])
            return v

        xz = cut(OA, NT * D, NT)
        hT = cut(OB, KD * KEYS, KD)
        win = cut(OC, KD * IN_COLS, KD)
        ada_at = [OD, OD + 2048] + [OB + 2048 * n for n in range(5)] + [OF]
        ada = [cut(at, KD * 256, KD) for at in ada_at]
        sig = cut(OA + 5120, 1024, 2)
        junk = cut(OA + 4608, 256)
        qkv = cut(OE, NT * QKV, NT)
        ada_acc = [cut(at + 256 * n, 256) for at, count in ((OE + NT * QKV, 3), (OD + 4096, 3))
                   for n in range(count)]
        mrow = cut(OE, 2 * D)
        ada_ones = cut(OE + NT * QKV + 3 * 256, P)
        qcT = cut(OF, 2 * SEQ, 2)
        kvT = cut(OF + 2048, KEYS)
        wuq = cut(OF + 3328, 2 * HEADS * HD, 2)
        wukv = cut(OF + 4864, D)
        uconv = cut(OF + 5888, 2 * (SEQ + 2 * CPAD), 2)
        upool = cut(OA, 2 * (SEQ + 2 * PPAD), 2)
        ptmp = cut(OA + 2080, 2 * (SEQ + 2 * PPAD), 2)
        mixT = cut(OA, KD * SEQ, KD)
        pdif = cut(OA + 6 * SEQ, 2 * SEQ, 2)
        yconv = cut(OA + KD * SEQ, 2 * SEQ, 2)
        KT_hi = [part(OB + KEYS * n, KEYS) for n in range(2)]
        QT_hi = [part(OB + 2560 + 2 * SEQ * n, 2 * SEQ, 2) for n in range(2)]
        QT_lo = [part(OC + 3328 * n, 2 * SEQ, 2) for n in range(2)]
        KT_lo = [part(OC + 3328 * n + 2 * SEQ, KEYS) for n in range(2)]
        probs = cut(OB + 6656, 2 * KEYS, 2)
        Opair = [cut(OC + 8192, SEQ, LT), cut(OB + 9216, SEQ, LT)]
        wout = cut(OC, KD * D, KD)
        probsT = cut(OD, 2 * KEYS, 2, NT)
        qraw = cut(OD + 2560, 2 * LT * HD, 2, LT)
        qrot = cut(OD + 4096, LT * HD, LT)
        V = cut(OE, NT * HEADS * VD, NT)
        ytok = cut(OF + 5888, LT * CW, LT)
        z1 = cut(OB, LT * D, LT)
        ln_rows = cut(OB + LT * D, 2 * D, 2)
        slot0 = OD
        zst = cut(OD + 6144, 2 * D, 2)
        ztmp = cut(OD + 8192, D)
        silS = cut(OD + 9216, 512)
        hmS = cut(OA + 8192, 2 * 512, 2)
        h2T = cut(OF, KD * SEQ, KD)
        slots = [slot0, OA, OC + 2048, OF]
        wg = [cut(s, 2048, KD) for s in slots]
        wu = [cut(s + 2048, 2048, KD) for s in slots]
        wd = [cut(s + 4096, 2048, 2) for s in slots]
        xe = cut(OA + 6144, D)
        xeT = cut(OA + 7168, D, KD)
        ye = cut(OA + 8192, D)
        hmE = cut(OA + 9216, 256, 2)
        silE = cut(OA + 9472, 256, 2)
        wd_hi, wd_lo = (part(OB + 2048 * n, 2048, 2) for n in range(2))
        hm_hi, hm_lo = (part(OB + 4096 + 256 * n, 256, 2) for n in range(2))
        ln2_rows = cut(OC, 2 * D, 2)
        chosen = cut(OA + 6144, TOPK * LT * E, TOPK, LT)
        score = cut(OA + 7168, LT * E, LT)
        sel = cut(OA + 7424, LT * E, LT)
        rt = cut(OA + 7680, LT * E, LT)
        member = arena[:, OA + 7936:OA + 7936 + LT * E // 2].bitcast(BF16).rearrange("p (t e) -> p t e", t=LT)
        small = cut(OB + LT * D, 512, 16)
        nb_tab = sb("nb_tab", [P, 2 * E + 1], I32)
        weight = sb("weight", [P, TOPK, LT])
        NB = BLOCKS + 2
        place_hot = [cut(OD + 6144 + D * n, LT * P, LT) for n in range(2)]
        block_hot = [cut(at, LT * 2 * NB, LT, 2) for at in (OB + LT * D + 512, OA + 6144)]
        logitsT = arena[0:E, OA + 9216:OA + 9216 + SEQ]
        exact = cut(OC + 8192, P).bitcast(BF16)
        ids = sb("ids", [P, NB], I32)
        wts = sb("wts", [P, BLOCKS + LT])
        id_in, id_out, w_now = sb("id_in", [P, 1], I32), sb("id_out", [P, 1], I32), sb("w_now", [P, 1])
        rw = sb("rw", [P, KD, E])
        rb = sb("rb", [P, E])
        pw = cut(OF + 5888, 2 * CW, 2)

        cst = sb("cst", [P, N_CONST])
        rows = sb("rows", [P, P])
        col = sb("col", [P, N_ROWS])
        sc = sb("sc", [P, 16])
        mod1 = sb("mod1", [P, 2, KD, 2])
        mod2 = sb("mod2", [P, 2, KD])
        gates = sb("gates", [P, 2, D])
        stats = sb("stats", [P, 2, 6])
        mv = sb("mv", [P, NT, 2])
        rstd = sb("rstd", [P, NT])
        ssq = sb("ssq", [P, NT, 2])
        rq = sb("rq", [P, NT, 2])
        mhalf = sb("mhalf", [P, 2 * NT])
        rtmp = sb("rtmp", [P, 4, 128])
        nmax = sb("nmax", [P, 4])
        rsum = sb("rsum", [P, 4])
        rinv = sb("rinv", [P, 2])
        bdiag = sb("bdiag", [P, 2, P])
        mark = sb("mark", [P, 2])
        shift5 = sb("shift5", [P, LT])
        ones_t = rtmp[:, 0, :]
        psum = stack.enter_context(nc.psum_tensor("psum", [P, 8 * 512], F32))

        def bank(b, n=512, at=0):
            return psum[:, b * 512 + at:b * 512 + at + n]

        ident = cst[:, C_ID:C_ID + P]

        ring, groups = stage1_jobs()
        slots_at = attention_slots()

        consts_in, rows_in, x_in = sem("consts_in"), sem("rows_in"), [sem(f"x_in{g}") for g in range(3)]
        ada_in = [sem(f"ada_in{n}") for n in range(8)]
        win_in, win2_in, gates_in = sem("win_in"), sem("win2_in"), sem("gates_in")
        wq_in, wout_in = sem("wq_in"), sem("wout_in")
        job_done = sem("job_done")
        emptied = {"act": sem("emptied_act"), "dve": sem("emptied_dve")}
        ada_used = sem("ada_used")
        ada_summed = sem("ada_summed")
        mod_sum = sem("mod_sum")
        mod_rows = sem("mod_rows")
        mod_ready = sem("mod_ready")
        silu_ready = sem("silu_ready")
        var_ready, rstd_ready, z_ready = sem("var_ready"), sem("rstd_ready"), sem("z_ready")
        ssq_ready, rq_ready, lat_ready = sem("ssq_ready"), sem("rq_ready"), sem("lat_ready")
        kr_ready = sem("kr_ready")
        dve_step, pool_step = sem("dve_step"), sem("pool_step")
        pads_ready, zeros_ready, diag_in = sem("pads_ready"), sem("zeros_ready"), sem("diag_in")
        pdif_ready = sem("pdif_ready")
        scores_ready, nmax_ready, probs_ready = sem("scores_ready"), sem("nmax_ready"), sem("probs_ready")
        filled = {"a": sem("filled_a"), "b": sem("filled_b")}
        cleared = {"a": sem("cleared_a"), "b": sem("cleared_b")}
        O_ready, O_kept = sem("O_ready"), sem("O_kept")
        rope_ready, odd_rope = sem("rope_ready"), sem("odd_rope")
        conv_ready, ytok_ready = sem("conv_ready"), sem("ytok_ready")
        stored = sem("stored")

        SLOT_BANK = {"a": 5, "b": 6}
        slot_no, n_slots = {}, {"a": 0, "b": 0}
        for name, b in prep_slots(0):
            n_slots[b] += 1
            slot_no[name] = (b, n_slots[b])
        for s in slots_at:
            for name, b in s:
                n_slots[b] += 1
                slot_no[name] = (b, n_slots[b])

        def job_emptied(eng, name):
            _, e, n = ring.of[name]
            eng.wait_ge(emptied[e], n)

        def slot_cleared(eng, name):
            b, n = slot_no[name]
            eng.wait_ge(cleared[b], n)

        def chain(eng, s, count, ins):
            count[0] += 1
            ins.then_inc(s, 1)
            eng.wait_ge(s, count[0])

        block = stack.enter_context(nc.Block())

        ADA_PIECES = [("col", 0, q) for q in range(8)] + [("gate", m, q) for m in range(2) for q in range(4)] \
            + [("col", 1, q) for q in range(8)]
        def ada_col(p):
            kind, m, q = p
            if kind == "col":
                return 3 * D * m + 256 * q
            return (2 * D if m == 0 else 5 * D) + 256 * q

        RV = lambda v, n: v.rearrange("(r q) -> r q", q=P)

        misc_in, pw_in = sem("misc_in"), sem("pw_in")
        x2_in = [sem(f"x2_in{t}") for t in range(LT)]
        ln1_in, shared_in, ln2_in, fills_in = sem("ln1_in"), sem("shared_in"), sem("ln2_in"), sem("fills_in")
        yact_ready = sem("yact_ready")
        proj_done, proj_used = sem("proj_done"), sem("proj_used")
        var3, rstd3, norm3, gain3, zst_ready = (sem(n) for n in ("var3", "rstd3", "norm3", "gain3", "zst_ready"))
        zn_out = [sem("zn_out0"), sem("zn_out1")]
        zT_done, zT_kept = sem("zT_done"), sem("zT_kept")
        up_done, sil_ready, hm_ready = sem("up_done"), sem("sil_ready"), sem("hm_ready")
        wd_gated = sem("wd_gated")
        down_done, down_used, acc_out = sem("down_done"), sem("down_used"), sem("acc_out")
        logits_done, score_ready, member_ready, pos_done, slots_ready = (
            sem(n) for n in ("logits_done", "score_ready", "member_ready", "pos_done", "slots_ready"))
        logitsT_done, logitsT_kept, exact_ready = (sem(n) for n in ("logitsT_done", "logitsT_kept", "exact_ready"))
        hot_ready, hot_used, ids_ready = (sem(n) for n in ("hot_ready", "hot_used", "ids_ready"))
        weights_in = [sem(f"weights_in{n}") for n in range(4)]
        gathered, xT_done, xT_act, xT_dve = (sem(n) for n in ("gathered", "xT_done", "xT_act", "xT_dve"))
        eup_done, esil, ehm, edown, y_ready, scattered, w_ready = (
            sem(n) for n in ("eup_done", "esil", "ehm", "edown", "y_ready", "scattered", "w_ready"))
        id_step = sem("id_step")
        whi_ready, wlo_ready, hm_step = sem("whi_ready"), sem("wlo_ready"), sem("hm_step")
        acc_in = [sem(f"acc_in{t}") for t in range(LT)]
        var5, rstd5, norm5, gain5, final_ready = (sem(n) for n in ("var5", "rstd5", "norm5", "gain5", "final_ready"))

        MINE = 256
        HALVES = [slice(0, 512), slice(512, D)]

        def wout_chunks(sp, a, b):
            sp.dma_start(wout[:, a:b, :], w_out[a * P:b * P, :].rearrange("(k p) f -> p k f", p=P)).then_inc(wout_in, 16)

        def stage3_loads(sp):
            sp.dma_start(rw[:, :, :], router_w.rearrange("(k p) e -> p k e", p=P)).then_inc(misc_in, 16)
            sp.dma_start(rb[:, :], router_bias.partition_broadcast(P)).then_inc(misc_in, 16)
            sp.dma_start(zn_dram[SEQ:SEQ + P, :], zero_rows).then_inc(fills_in, 16)
            sp.dma_start(acc_dram[SEQ:SEQ + P, :], zero_rows).then_inc(fills_in, 16)
            sp.wait_ge(scores_ready, UNITS - LT)
            wout_chunks(sp, 0, 3)
            b, n = slot_no[("yT", 1, 1)]
            sp.wait_ge(filled[b], n)
            sp.dma_start(pw, conv_pw.rearrange("(k p) f -> p k f", p=P)).then_inc(pw_in, 16)
            sp.wait_ge(scores_ready, UNITS)
            wout_chunks(sp, 3, 7)
            for b in "ab":
                sp.wait_ge(filled[b], n_slots[b])
            sp.wait_ge(probs_ready, UNITS)
            for t in range(LT):
                sp.dma_start(z1[:, t, :], x[0, t * P:(t + 1) * P, :]).then_inc(x2_in[t], 16)
                if t == 0:
                    sp.dma_start(ln_rows[:, 0, :], ln1_g.partition_broadcast(P)).then_inc(ln1_in, 16)
                    sp.dma_start(ln_rows[:, 1, :], ln1_b.partition_broadcast(P)).then_inc(ln1_in, 16)
            for dst, src in ((wg[0], sh_wg), (wu[0], sh_wu), (wd[0], sh_wd)):
                sp.dma_start(dst, src.rearrange("(k p) f -> p k f", p=P)).then_inc(shared_in, 16)
            for t in range(LT):
                sp.wait_ge(zst_ready, t + 1)
                sp.dma_start(zn_dram[t * P:(t + 1) * P, :], zst[:, t % 2, :]).then_inc(zn_out[t % 2], 16)

            def expert(e, slot, which=(0, 1, 2)):
                for n in which:
                    dst, src = ((wg[slot], exp_wg), (wu[slot], exp_wu), (wd[slot], exp_wd))[n]
                    sp.dma_start(dst, src[e].rearrange("(k p) f -> p k f", p=P)).then_inc(weights_in[slot], 16)

            sp.wait_ge(proj_done, LT)
            expert(0, 1)
            expert(1, 2)
            sp.dma_start(ln2_rows[:, 0, :], ln2_g.partition_broadcast(P)).then_inc(ln2_in, 16)
            sp.dma_start(ln2_rows[:, 1, :], ln2_b.partition_broadcast(P)).then_inc(ln2_in, 16)
            for t in range(LT):
                if t == 4:
                    sp.wait_ge(up_done, 4)
                    expert(2, 3)
                    expert(3, 0, (0, 1))
                sp.wait_ge(down_used, 2 * t + 2)
                sp.dma_start(acc_dram[t * P:(t + 1) * P, :], z1[:, t, :]).then_inc(acc_out, 16)
            sp.wait_ge(down_done, 2 * LT)
            expert(3, 0, (2,))
            with sp.Fori(1, E // 4) as g:
                for s in range(4):
                    before = sp.value_load(nb_tab[0:1, bass.ds(E + 4 * (g - 1) + s + 1, 1)], min_val=1, max_val=BLOCKS)
                    sp.wait_ge(edown, before + 1)
                    expert(4 * g + s, (s + 1) % 4)
            total = sp.value_load(nb_tab[0:1, 2 * E:2 * E + 1], min_val=1, max_val=BLOCKS)
            sp.wait_ge(scattered, total * 16 + 16)
            for t in range(LT):
                sp.dma_start(z1[:, t, :], acc_dram[t * P:(t + 1) * P, :]).then_inc(acc_in[t], 16)
            for t in range(LT):
                sp.wait_ge(final_ready, t + 1)
                sp.dma_start(out[0, t * P:(t + 1) * P, :], z1[:, t, :]).then_inc(stored, 16)
            sp.wait_ge(stored, 16 * LT)

        def stage3_tensor(pe):
            pe.wait_ge(wout_in, 48)
            for b in "ab":
                pe.wait_ge(cleared[b], n_slots[b])

            def project(i):
                b0 = 2 * (i % 2)
                if i >= 2:
                    pe.wait_ge(proj_used, i - 1)
                for h in range(2):
                    for k in range(KD):
                        mm = nc.tensor.matmul(bank(b0 + h), mixT[:, k, i * P:(i + 1) * P], wout[:, k, HALVES[h]],
                                              start=k == 0, stop=k == KD - 1)
                mm.then_inc(proj_done, 1)

            def turn(i):
                pe.wait_ge(zst_ready, i + 1)
                if i >= 1:
                    pe.wait_ge(zT_kept, i)
                for k in range(KD):
                    mm = nc.tensor.transpose(bank(5 + k // 4, P, (k % 4) * P), zst[:, i % 2, k * P:(k + 1) * P], ident)
                mm.then_inc(zT_done, 1)

            for i in range(LT):
                project(i)
                if i >= 1:
                    turn(i - 1)

            def shared_up(n, f):
                if n == 1:
                    pe.wait_ge(hm_ready, f + 1)
                for m, w in ((0, wg[0]), (1, wu[0])):
                    for k in range(KD):
                        mm = nc.tensor.matmul(bank(2 * f + m), w[:, k, f * P:(f + 1) * P], h2T[:, k, HALVES[n]],
                                              start=k == 0, stop=k == KD - 1)
                mm.then_inc(up_done, 1)

            def shared_down(n, first=0, last=8):
                pe.wait_ge(hm_ready, 2 * n + 2)
                pe.wait_ge(wd_gated, 1)
                for r in range(first, last):
                    t, h, q = r // 2, r % 2, 8 * n + r
                    if q >= 3:
                        pe.wait_ge(down_used, q - 2)
                    for k in range(2):
                        mm = nc.tensor.matmul(bank(4 + q % 3), hmS[:, k, t * P:(t + 1) * P], wd[0][:, k, HALVES[h]],
                                              start=k == 0, stop=k == 1)
                    mm.then_inc(down_done, 1)

            def logits(n):
                pe.wait_ge(misc_in, 32)
                for k in range(KD):
                    mm = nc.tensor.matmul(bank(7 - 3 * n)[0:E, :], rw[:, k, :], h2T[:, k, HALVES[n]], start=k == 0, stop=k == KD - 1)
                mm.then_inc(logitsT_done, 1)

            pe.wait_ge(shared_in, 48)
            pe.wait_ge(proj_used, LT)
            pe.wait_ge(zT_kept, 4)
            shared_up(0, 0)
            shared_up(0, 1)
            turn(LT - 1)
            logits(0)
            pe.wait_ge(zT_kept, LT)
            logits(1)
            pe.wait_ge(logitsT_kept, 2)
            for i in range(LT):
                mm = nc.tensor.transpose(bank(7, E, i * E), logitsT[:, i * P:(i + 1) * P], ident[0:E, 0:E])
            mm.then_inc(logits_done, 1)
            shared_down(0)
            shared_up(1, 0)

            pe.wait_ge(member_ready, 1)
            pe.wait_ge(exact_ready, 1)
            tri, ones = exact[:, 0:P], exact[:, P:2 * P]
            for i in range(LT):
                for j in range(i + 1):
                    nc.tensor.matmul(bank(7, E, i * E), tri if j == i else ones, member[:, j, :], start=j == 0, stop=j == i)
            for j in range(LT):
                mm = nc.tensor.matmul(bank(7, E, LT * E), ones, member[:, j, :], start=j == 0, stop=j == LT - 1)
            mm.then_inc(pos_done, 1)
            shared_up(1, 1)
            for n in range(TOPK * LT):
                k, t = n // LT, n % LT
                pe.wait_ge(hot_ready, k + 1)
                nc.tensor.matmul(bank(7, 2 * NB), place_hot[k % 2][:, t, :], block_hot[k % 2][:, t, :, :].rearrange("p a b -> p (a b)"),
                                 start=n == 0, stop=n == TOPK * LT - 1).then_inc(hot_used, 1)
                if n == LT - 1:
                    shared_down(1, 0, 3)
            shared_down(1, 3, 8)

            def turn_rows(first=False):
                for k in range(KD):
                    mm = nc.tensor.transpose(bank(2 + k // 4, P, (k % 4) * P), xe[:, k * P:(k + 1) * P], ident)
                    if first and k == 0:
                        mm.then_inc(edown, 1)
                mm.then_inc(xT_done, 1)

            pe.wait_ge(gathered, 16)
            turn_rows(first=True)
            with pe.Fori(0, E // 4) as g:
                for s in range(4):
                    slot = (s + 1) % 4
                    pe.wait_ge(weights_in[slot], g * 48 + 48)
                    n = pe.value_load(nb_tab[0:1, bass.ds(4 * g + s, 1)], min_val=1, max_val=LT)
                    first = pe.value_load(nb_tab[0:1, bass.ds(E + 4 * g + s, 1)], min_val=0, max_val=BLOCKS - 1)
                    with pe.Fori(0, n) as j:
                        pe.wait_ge(xT_act, first + j + 1)
                        pe.wait_ge(xT_dve, first + j + 1)
                        for f in range(2):
                            for m, w in ((0, wg[slot]), (1, wu[slot])):
                                for k in range(KD):
                                    mm = nc.tensor.matmul(bank(f, P, m * P), w[:, k, f * P:(f + 1) * P], xeT[:, k, :],
                                                          start=k == 0, stop=k == KD - 1)
                            mm.then_inc(eup_done, 1)
                        pe.wait_ge(gathered, (first + j) * 16 + 32)
                        turn_rows()
                        pe.wait_ge(wlo_ready, 4 * g + s + 1)
                        for k in range(2):
                            pe.wait_ge(ehm, (first + j) * 2 + k + 1)
                            for h in range(2):
                                for term, (a, w) in enumerate(((hm_hi, wd_hi), (hm_hi, wd_lo), (hm_lo, wd_hi))):
                                    mm = nc.tensor.matmul(bank(4 + h), a[:, k, :], w[:, k, HALVES[h]],
                                                          start=k == 0 and term == 0, stop=k == 1 and term == 2)
                        mm.then_inc(edown, 1)

        def stage3_scalar(act):
            def keep_turn(i):
                act.wait_ge(zT_done, i + 1)
                for k in range(KD):
                    ins = nc.scalar.activation(h2T[:, k, i * P:(i + 1) * P], bank(5 + k // 4, P, (k % 4) * P), ACT.Identity,
                                               bias=mod2[:, 0, k:k + 1], scale=mod2[:, 1, k:k + 1])
                ins.then_inc(zT_kept, 1)

            def gate(n):
                for f in range(2):
                    act.wait_ge(up_done, 2 * n + f + 1)
                    if 2 * n + f >= 1:
                        act.wait_ge(hm_ready, 2 * n + f)
                    nc.scalar.activation(silS, bank(2 * f), ACT.Silu).then_inc(sil_ready, 1)

            for i in range(LT - 1):
                keep_turn(i)
            gate(0)
            keep_turn(LT - 1)
            for n in range(2):
                act.wait_ge(logitsT_done, n + 1)
                nc.scalar.copy(logitsT[:, HALVES[n]], bank(7 - 3 * n)[0:E, :]).then_inc(logitsT_kept, 1)
            act.wait_ge(logits_done, 1)
            nc.scalar.activation(score.rearrange("p t e -> p (t e)"), bank(7, LT * E), ACT.Sigmoid).then_inc(score_ready, 1)
            gate(1)

            def keep_rows():
                for k in range(4, KD):
                    ins = nc.scalar.activation(xeT[:, k, :], bank(3, P, (k - 4) * P), ACT.Identity,
                                               bias=mod2[:, 0, k:k + 1], scale=mod2[:, 1, k:k + 1])
                ins.then_inc(xT_act, 1)

            act.wait_ge(ids_ready, 1)
            act.wait_ge(xT_done, 1)
            keep_rows()
            act.wait_ge(acc_out, 16 * LT)
            with act.Fori(0, E // 4) as g:
                for s in range(4):
                    slot = (s + 1) % 4
                    n = act.value_load(nb_tab[0:1, bass.ds(4 * g + s, 1)], min_val=1, max_val=LT)
                    first = act.value_load(nb_tab[0:1, bass.ds(E + 4 * g + s, 1)], min_val=0, max_val=BLOCKS - 1)
                    act.wait_ge(weights_in[slot], g * 48 + 48)
                    act.wait_ge(edown, first + 1)
                    for k in range(2):
                        nc.scalar.copy(wd_hi[:, k, :], wd[slot][:, k, :]).then_inc(whi_ready, 1)
                    with act.Fori(0, n) as j:
                        for f in range(2):
                            act.wait_ge(eup_done, (first + j) * 2 + f + 1)
                            nc.scalar.activation(silE[:, f, :], bank(f, P), ACT.Silu).then_inc(esil, 1)
                        act.wait_ge(xT_done, (first + j) + 2)
                        keep_rows()
            for i in range(LT):
                z = z1[:, i, :]
                act.wait_ge(rstd5, i + 1)
                nc.scalar.activation(z, z, ACT.Identity, bias=shift5[:, i:i + 1], scale=rstd[:, i:i + 1]).then_inc(norm5, 1)

        def stage3_vector(dve, then):
            dve.wait_ge(ln1_in, 32)
            for i in range(LT):
                z = z1[:, i, :]
                dve.wait_ge(proj_done, i + 1)
                nc.vector.tensor_tensor(ztmp, psum[:, 1024 * (i % 2):1024 * (i % 2) + D], gates[:, 0, :], ALU.mult)\
                    .then_inc(proj_used, 1)
                dve.wait_ge(proj_used, i + 1)
                dve.wait_ge(x2_in[i], 16)
                then(nc.vector.scalar_tensor_tensor(z, z, ALPHA, ztmp, ALU.mult, ALU.add))
                for part in range(2):
                    if part:
                        dve.wait_ge(gain3, i + 1)
                    for s in range(2):
                        then(nc.vector.bn_stats(stats[:, s, :], z[:, s * 512:(s + 1) * 512]))
                    nc.vector.bn_aggr(mv[:, i, :], stats[:, :, :].rearrange("p a b -> p (a b)")).then_inc(var3, 1)
                    dve.wait_ge(rstd3, 2 * i + part + 1)
                    if part == 0:
                        nc.vector.tensor_scalar(z, z, mv[:, i, 0:1], rstd[:, i:i + 1], ALU.subtract, ALU.mult).then_inc(norm3, 1)
                    else:
                        if i >= 2:
                            dve.wait_ge(zn_out[i % 2], 16 * (i // 2))
                            dve.wait_ge(zT_done, i - 1)
                        nc.vector.tensor_scalar(zst[:, i % 2, :], z, mv[:, i, 0:1], rstd[:, i:i + 1],
                                                ALU.subtract, ALU.mult).then_inc(zst_ready, 1)

            def hidden(n, f):
                if n == 1 and f == 0:
                    dve.wait_ge(down_done, 8)
                dve.wait_ge(sil_ready, 2 * n + f + 1)
                nc.vector.tensor_tensor(hmS[:, f, :], bank(2 * f + 1), silS, ALU.mult).then_inc(hm_ready, 1)

            def start_sums(n, first=0, last=8):
                for r in range(first, last):
                    q = 8 * n + r
                    dve.wait_ge(down_done, q + 1)
                    z = z1[:, 4 * n + r // 2, HALVES[r % 2]]
                    nc.vector.scalar_tensor_tensor(z, z, ALPHA, bank(4 + q % 3), ALU.mult, ALU.add).then_inc(down_used, 1)

            hidden(0, 0)
            hidden(0, 1)

            V = nc.vector
            tt, ts, stt, red = V.tensor_tensor, V.tensor_scalar, V.scalar_tensor_tensor, V.tensor_reduce
            S = lambda n: small[:, n, :]
            S8 = lambda n, m=0: small[:, n, 8 * m:8 * m + 8]
            by_group = lambda v: v.rearrange("p t (g e) -> p (t g) e", g=GROUPS)
            over8 = lambda v: v.unsqueeze(2).to_broadcast([P, 32, GE])
            over32 = lambda v: v.unsqueeze(2).to_broadcast([P, LT, E])
            dve.wait_ge(score_ready, 1)
            then(tt(sel, score, rb[:, :].unsqueeze(1).to_broadcast([P, LT, E]), ALU.add))
            then(red(S(0), by_group(sel), AX.X, ALU.max))
            then(tt(by_group(rt), by_group(sel), over8(S(0)), ALU.is_equal))
            then(red(S(1), by_group(rt), AX.X, ALU.add))
            then(stt(by_group(rt), by_group(rt), -BIG, by_group(sel), ALU.mult, ALU.add))
            then(red(S(2), by_group(rt), AX.X, ALU.max))
            then(ts(S(1), S(1), 1.5, 1.0, ALU.is_gt, ALU.subtract))
            then(stt(S(1), S(1), BIG, S(0), ALU.mult, ALU.add))
            then(tt(S(2), S(2), S(1), ALU.max))
            then(tt(S(3), S(0), S(2), ALU.add))
            start_sums(0, 0, 2)
            gs = S(3).rearrange("p (t g) -> p t g", g=GROUPS)
            other = gs.unsqueeze(2).to_broadcast([P, LT, GROUPS, GROUPS])
            own = gs.unsqueeze(3).to_broadcast([P, LT, GROUPS, GROUPS])
            grid = lambda v: v.rearrange("p (t g j) -> p t g j", t=LT, g=GROUPS)
            ga = rt.rearrange("p t e -> p (t e)")[:, 0:128]
            gb = rt.rearrange("p t e -> p (t e)")[:, 128:256]
            mask = lambda at: cst[:, at:at + 16].unsqueeze(1).to_broadcast([P, LT, 16])
            flat = lambda v: v.rearrange("p (t g) -> p t g", t=LT)
            then(tt(grid(ga), other, own, ALU.is_gt))
            then(tt(grid(gb), other, own, ALU.is_ge))
            then(tt(flat(ga), flat(ga), mask(C_GT), ALU.mult))
            then(tt(flat(gb), flat(gb), mask(C_GE), ALU.mult))
            then(tt(ga, ga, gb, ALU.add))
            then(red(S(1), ga.rearrange("p (g j) -> p g j", j=GROUPS), AX.X, ALU.add))
            then(ts(S(1), S(1), 1.5, 1.0, ALU.is_lt, ALU.subtract))
            then(stt(by_group(sel), over8(S(1)), BIG, by_group(sel), ALU.mult, ALU.add))
            start_sums(0, 2, 4)
            iota = cst[:, C_IOTA:C_IOTA + E].unsqueeze(1).to_broadcast([P, LT, E])
            for k in range(TOPK):
                then(red(S8(4), sel, AX.X, ALU.max))
                then(tt(rt, sel, over32(S8(4)), ALU.is_equal))
                then(tt(rt, rt, iota, ALU.mult))
                then(red(S8(4, 1), rt, AX.X, ALU.min))
                then(tt(chosen[:, k], iota, over32(S8(4, 1)), ALU.is_equal))
                then(stt(sel, chosen[:, k], -BIG, sel, ALU.mult, ALU.add))
                start_sums(0, 4 + k, 5 + k)
            then(tt(member, chosen[:, 0], chosen[:, 1], ALU.add))
            then(tt(rt, chosen[:, 2], chosen[:, 3], ALU.add))
            tt(member, member, rt, ALU.add).then_inc(member_ready, 1)
            dve.wait_ge(member_ready, 1)
            for k in range(TOPK):
                then(tt(rt, chosen[:, k], score, ALU.mult))
                then(red(S8(5, k), rt, AX.X, ALU.add))
            then(red(S8(6), S(5).rearrange("p (k t) -> p t k", k=TOPK), AX.X, ALU.add))
            then(V.reciprocal(S8(6, 1), S8(6)))
            then(ts(S8(6, 1), S8(6, 1), ROUTED_SCALE, None, ALU.mult))
            then(tt(weight[:, :, :], S(5).rearrange("p (k t) -> p k t", k=TOPK),
                    S8(6, 1).unsqueeze(1).to_broadcast([P, TOPK, LT]), ALU.mult))
            hidden(1, 0)
            dve.wait_ge(pos_done, 1)
            si = small[:, 7, :].bitcast(I32)
            then(ts(si, bank(7, E, LT * E), float(P - 1), None, ALU.add))
            then(ts(si, si, 7, None, ALU.logical_shift_right))
            then(ts(nb_tab[:, 0:E], si, 1, None, ALU.max))
            then(V.tensor_copy(S(8), nb_tab[:, 0:E]))
            then(V.tensor_copy(S(9), S(8)))
            a, b = 9, 10
            for d in (1, 2, 4, 8, 16):
                then(V.tensor_copy(S(b)[:, 0:d], S(a)[:, 0:d]))
                then(tt(S(b)[:, d:E], S(a)[:, d:E], S(a)[:, 0:E - d], ALU.add))
                a, b = b, a
            then(V.tensor_copy(nb_tab[:, 2 * E:2 * E + 1], S(a)[:, E - 1:E]))
            then(tt(S(11), S(a), S(8), ALU.subtract))
            then(V.tensor_copy(nb_tab[:, E:2 * E], S(11)))
            then(stt(sel, S(11).unsqueeze(1).to_broadcast([P, LT, E]), float(P),
                     bank(7, LT * E).rearrange("p (t e) -> p t e", e=E), ALU.mult, ALU.add))
            for k in range(TOPK):
                then(tt(rt, chosen[:, k], sel, ALU.mult))
                then(red(S8(12, k), rt, AX.X, ALU.add))
            place_i, blk_i = small[:, 13, :].bitcast(I32), small[:, 14, :].bitcast(I32)
            place, blk, token = 9, 10, 15
            then(V.tensor_copy(si, S(12)))
            then(ts(place_i, si, P - 1, None, ALU.bitwise_and))
            then(ts(blk_i, si, 7, None, ALU.logical_shift_right))
            then(V.tensor_copy(S(place), place_i))
            then(V.tensor_copy(S(blk), blk_i))
            tok = cst[:, C_TOK:C_TOK + LT].unsqueeze(1).to_broadcast([P, TOPK, LT])
            stt(S(token).rearrange("p (k t) -> p k t", k=TOPK), S(place).rearrange("p (k t) -> p k t", k=TOPK),
                float(SEQ), tok, ALU.add, ALU.subtract).then_inc(slots_ready, 1)
            dve.wait_ge(slots_ready, 1)
            for z in zn_out:
                dve.wait_ge(z, 64)
            dve.wait_ge(zT_done, LT)
            iota_p = cst[:, C_POS:C_POS + P].unsqueeze(1).to_broadcast([P, LT, P])
            iota_b = cst[:, C_POS:C_POS + NB].unsqueeze(1).to_broadcast([P, LT, NB])
            for k in range(TOPK):
                if k >= 2:
                    dve.wait_ge(hot_used, (k - 1) * LT)
                of_k = lambda v, n: v.unsqueeze(2).to_broadcast([P, LT, n])
                hot, row = block_hot[k % 2], slice(LT * k, LT * (k + 1))
                tt(place_hot[k % 2], iota_p, of_k(S(place)[:, row], P), ALU.is_equal)
                then(tt(hot[:, :, 1, :], iota_b, of_k(S(blk)[:, row], NB), ALU.is_equal))
                then(tt(hot[:, :, 0, :], hot[:, :, 1, :], of_k(S(token)[:, row], NB), ALU.mult))
                tt(hot[:, :, 1, :], hot[:, :, 1, :], of_k(weight[:, k, :], NB), ALU.mult).then_inc(hot_ready, 1)
                if k == 0:
                    hidden(1, 1)
                elif k == 1:
                    start_sums(1, 0, 2)
            dve.wait_ge(hot_used, TOPK * LT)
            then(ts(ids[:, :], bank(7, NB), -1.0, cst[:, C_SPARE:C_SPARE + 1], ALU.mult, ALU.add))
            V.tensor_copy(wts[:, 0:NB], bank(7, NB, NB)).then_inc(ids_ready, 1)
            start_sums(1, 2)

            def keep_rows():
                for k in range(4):
                    ins = nc.vector.tensor_scalar(xeT[:, k, :], bank(2, P, k * P), mod2[:, 1, k:k + 1], mod2[:, 0, k:k + 1],
                                                  ALU.mult, ALU.add)
                ins.then_inc(xT_dve, 1)

            dve.wait_ge(ids_ready, 1)
            dve.wait_ge(xT_done, 1)
            keep_rows()
            dve.wait_ge(acc_out, 16 * LT)
            V.memset(w_now[:, :], 0.0).then_inc(y_ready, 1)
            with dve.Fori(0, E // 4) as g:
                for s in range(4):
                    slot = (s + 1) % 4
                    n = dve.value_load(nb_tab[0:1, bass.ds(4 * g + s, 1)], min_val=1, max_val=LT)
                    first = dve.value_load(nb_tab[0:1, bass.ds(E + 4 * g + s, 1)], min_val=0, max_val=BLOCKS - 1)
                    for k in range(2):
                        dve.wait_ge(whi_ready, g * 8 + 2 * s + k + 1)
                        ins = tt(wd_lo[:, k, :], wd[slot][:, k, :], wd_hi[:, k, :].bitcast(F32), ALU.subtract)
                    ins.then_inc(wlo_ready, 1)
                    with dve.Fori(0, n) as j:
                        dve.wait_ge(y_ready, first + j + 1)
                        V.tensor_copy(w_now[:, :], wts[:, bass.ds(first + j, 1)]).then_inc(w_ready, 1)
                        for f in range(2):
                            dve.wait_ge(esil, (first + j) * 2 + f + 1)
                            tt(hmE[:, f, :], bank(f, P, P), silE[:, f, :], ALU.mult).then_inc(hm_step, 1)
                            dve.wait_ge(hm_step, (first + j) * 4 + 2 * f + 1)
                            V.tensor_copy(hm_hi[:, f, :], hmE[:, f, :]).then_inc(hm_step, 1)
                            dve.wait_ge(hm_step, (first + j) * 4 + 2 * f + 2)
                            tt(hm_lo[:, f, :], hmE[:, f, :], hm_hi[:, f, :].bitcast(F32), ALU.subtract).then_inc(ehm, 1)
                        dve.wait_ge(xT_done, first + j + 2)
                        keep_rows()
                        dve.wait_ge(edown, first + j + 2)
                        dve.wait_ge(scattered, (first + j) * 16 + 16)
                        dve.wait_ge(w_ready, first + j + 1)
                        for h in range(2):
                            ins = stt(ye[:, HALVES[h]], bank(4 + h), w_now[:, 0:1], gates[:, 1, HALVES[h]], ALU.mult, ALU.mult)
                        ins.then_inc(y_ready, 1)

            dve.wait_ge(ln2_in, 32)
            for i in range(LT + 1):
                if i < LT:
                    dve.wait_ge(acc_in[i], 16)
                    if i >= 1:
                        dve.wait_ge(var5, i)
                    for s in range(2):
                        then(nc.vector.bn_stats(stats[:, s, :], z1[:, i, s * 512:(s + 1) * 512]))
                    nc.vector.bn_aggr(mv[:, i, :], stats[:, :, :].rearrange("p a b -> p (a b)")).then_inc(var5, 1)
                if i >= 1:
                    z = z1[:, i - 1, :]
                    dve.wait_ge(norm5, i)
                    then(nc.vector.tensor_tensor(z, z, ln2_rows[:, 0, :], ALU.mult))
                    nc.vector.tensor_tensor(z[:, 0:MINE], z[:, 0:MINE], ln2_rows[:, 1, 0:MINE], ALU.add).then_inc(gain5, 1)

        def stage3_gpsimd(pool, then):
            def inv_root1(i):
                then(nc.gpsimd.tensor_scalar(rstd[:, i:i + 1], mv[:, i, 1:2], 1.0, EPS, ALU.mult, ALU.add))
                return nc.gpsimd.tensor_tensor(rstd[:, i:i + 1], rstd[:, i:i + 1], mhalf[:, 0:1], ALU.pow)

            then(nc.gpsimd.memset(ones_t[:, :], 1.0))
            pool.wait_ge(ln1_in, 32)
            for i in range(LT):
                z = z1[:, i, :]
                pool.wait_ge(var3, 2 * i + 1)
                inv_root1(i).then_inc(rstd3, 1)
                pool.wait_ge(norm3, i + 1)
                then(nc.gpsimd.tensor_tensor(z, z, ln_rows[:, 0, :], ALU.mult))
                nc.gpsimd.tensor_tensor(z, z, ln_rows[:, 1, :], ALU.add).then_inc(gain3, 1)
                if i == LT - 1:
                    pool.wait_ge(shared_in, 48)
                    nc.gpsimd.tensor_tensor(wd[0], wd[0], gates[:, 1, :].unsqueeze(1).to_broadcast([P, 2, D]), ALU.mult)\
                        .then_inc(wd_gated, 1)
                pool.wait_ge(var3, 2 * i + 2)
                inv_root1(i).then_inc(rstd3, 1)
            nc.gpsimd.tensor_copy(exact[:, 0:P], cst[:, C_TRI:C_TRI + P])
            nc.gpsimd.tensor_copy(exact[:, P:2 * P], ones_t[:, :]).then_inc(exact_ready, 1)
            pool.wait_ge(fills_in, 32)

            def carry(n):
                nc.gpsimd.tensor_tensor(mark[:, n:n + 1], ones_t[:, 0:1], ones_t[:, 0:1], ALU.mult)

            def fetch():
                nc.gpsimd.indirect_dma_start(
                    out=xe, out_offset=None, in_=zn_dram,
                    in_offset=bass.IndirectOffsetOnAxis(ap=id_in[:, 0:1], axis=0)).then_inc(gathered, 16)

            pool.wait_ge(ids_ready, 1)
            pool.wait_ge(zn_out[0], 64)
            pool.wait_ge(zn_out[1], 64)
            nc.gpsimd.dma_start(acc_dram[SEQ:SEQ + P, :], zero_rows).then_inc(scattered, 16)
            total = pool.value_load(nb_tab[0:1, 2 * E:2 * E + 1], min_val=1, max_val=BLOCKS)
            nc.gpsimd.tensor_copy(id_in[:, :], ids[:, 0:1]).then_inc(id_step, 1)
            pool.wait_ge(id_step, 1)
            fetch()
            pool.wait_ge(xT_done, 1)
            pool.wait_ge(gathered, 16)
            nc.gpsimd.tensor_copy(id_in[:, :], ids[:, 1:2]).then_inc(id_step, 1)
            pool.wait_ge(id_step, 2)
            fetch()
            pool.wait_ge(acc_out, 16 * LT)
            with pool.Fori(0, total) as b:
                pool.wait_ge(xT_done, b + 2)
                pool.wait_ge(gathered, b * 16 + 32)
                nc.gpsimd.tensor_copy(id_in[:, :], ids[:, bass.ds(b + 2, 1)]).then_inc(id_step, 1)
                pool.wait_ge(id_step, b * 2 + 3)
                carry(0)
                fetch()
                pool.wait_ge(scattered, b * 16 + 16)
                nc.gpsimd.tensor_copy(id_out[:, :], ids[:, bass.ds(b, 1)]).then_inc(id_step, 1)
                pool.wait_ge(id_step, b * 2 + 4)
                pool.wait_ge(y_ready, b + 2)
                carry(1)
                nc.gpsimd.indirect_dma_start(
                    out=acc_dram, out_offset=bass.IndirectOffsetOnAxis(ap=id_out[:, 0:1], axis=0),
                    in_=ye, in_offset=None, compute_op=ALU.add).then_inc(scattered, 16)
            pool.wait_ge(gathered, total * 16 + 32)
            carry(0)
            pool.wait_ge(ln2_in, 32)
            for i in range(LT + 1):
                if i < LT:
                    pool.wait_ge(var5, i + 1)
                    then(inv_root1(i))
                    nc.gpsimd.tensor_scalar(shift5[:, i:i + 1], mv[:, i, 0:1], -1.0, rstd[:, i:i + 1],
                                            ALU.mult, ALU.mult).then_inc(rstd5, 1)
                if i >= 1:
                    pool.wait_ge(gain5, i)
                    z = z1[:, i - 1, MINE:]
                    nc.gpsimd.tensor_tensor(z, z, ln2_rows[:, 1, MINE:], ALU.add).then_inc(final_ready, 1)

        @block.sync
        def _(sp):
            sp.dma_start(cst[:, :], const).then_inc(consts_in, 16)
            for at, n, src in ((R_C, 8, c[0]), (R_CC, 8, c_ctx), (R_MOD1, 16, ada_b[0:2 * D]),
                               (R_MOD2, 16, ada_b[3 * D:5 * D]), (R_PSC, 2, pool_scale), (R_CB, 2, conv_b),
                               (R_LG, 2, conv_ln_g), (R_LB, 2, conv_ln_b), (R_QG, 2, q_norm_g), (R_KVG, 1, kv_norm_g)):
                sp.dma_start(rows[at:at + n, :], RV(src, n)).then_inc(rows_in, 16)
            sp.dma_start(rows[R_DW:R_DW + 2 * TAPS, :],
                         conv_dw.rearrange("t (h q) -> (t h) q", q=P)).then_inc(rows_in, 16)
            sp.dma_start(xz[:, 0:CT, :], ctx[0].rearrange("(t p) d -> p t d", p=P)).then_inc(x_in[0], 16)

            def latent(g):
                a = (g - 1) * 4
                sp.dma_start(xz[:, CT + a:CT + a + 4, :],
                             x[0, a * P:(a + 4) * P].rearrange("(t p) d -> p t d", p=P)).then_inc(x_in[g], 16)

            def ada_piece(n):
                at = n if n < 8 else n % 2
                if n in (8, 9):
                    sp.wait_ge(ada_used, n - 7)
                if n >= 10:
                    sp.wait_ge(ada_summed, n - 9)
                a = ada_col(ADA_PIECES[n])
                sp.dma_start(ada[at], ada_w[:, a:a + 256].rearrange("(k p) f -> p k f", p=P))\
                    .then_inc(ada_in[at], 16)

            ada_piece(0)
            latent(1)
            ada_piece(1)
            latent(2)
            for n in range(2, 8):
                ada_piece(n)
            sp.dma_start(win[:, :, 0:QKV], w_in[:, 0:QKV].rearrange("(k p) f -> p k f", p=P)).then_inc(win_in, 16)
            for m in range(2):
                a = 2 * D if m == 0 else 5 * D
                sp.dma_start(gates[:, m, :], ada_b[a:a + D].partition_broadcast(P)).then_inc(gates_in, 16)
            sp.dma_start(win[:, :, QKV:IN_COLS], w_in[:, QKV:IN_COLS].rearrange("(k p) f -> p k f", p=P)).then_inc(win2_in, 16)
            sp.dma_start(wuq, w_uq.rearrange("(k p) f -> p k f", p=P)).then_inc(wq_in, 16)
            sp.dma_start(wukv, w_ukv).then_inc(wq_in, 16)
            sp.wait_ge(zeros_ready, 1)
            for g in range(4):
                o = PG * (g % 2)
                sp.dma_start(bdiag[o:o + PG, g // 2, o:o + PG], pool_w[g]).then_inc(diag_in, 16)
            for n in range(8, 24):
                ada_piece(n)
            sp.wait_ge(job_done, ring.of[("V", 0)][0])
            wout_chunks(sp, 7, 8)
            stage3_loads(sp)

        @block.tensor
        def _(pe):
            n_ring = [0]

            def ring_bank(name):
                n = ring.of[name][0]
                assert n == n_ring[0], name
                n_ring[0] += 1
                if n >= 4:
                    job_emptied(pe, ring.jobs[n - 4][0])
                return bank(n % 4)

            pe.wait_ge(consts_in, 16)
            pe.wait_ge(rows_in, 16 * 11)
            o = ring_bank(("rows",))
            nc.tensor.transpose(o[:, 0:N_ROWS], rows[0:N_ROWS, :], ident[0:N_ROWS, 0:N_ROWS]).then_inc(job_done, 1)

            pe.wait_ge(silu_ready, 1)
            pe.wait_ge(zeros_ready, 1)

            def mod_cols(r):
                pe.wait_ge(mod_rows, r + 1)
                for j in range(4 * r, 4 * r + 4):
                    mm = nc.tensor.transpose(bank(4, 2, 2 * j), mrow[0:2, j * P:(j + 1) * P], ident[0:2, 0:2])
                return mm

            for q in range(8):
                r = q // 2
                pe.wait_ge(ada_in[q], 16)
                if q == 6:
                    pe.wait_ge(mod_rows, 1)
                for k in range(KD):
                    mm = nc.tensor.matmul(bank(5 + r % 3, 256, 256 * (q % 2))[0:2, :], sc[:, k:16:8], ada[q][:, k, :],
                                          start=k == 0, stop=k == KD - 1)
                mm.then_inc(ada_used, 1)
                if q in (3, 5):
                    mod_cols(r - 1)
            mod_cols(2)
            mod_cols(3).then_inc(mod_sum, 1)

            def second_cols(q):
                n = 8 + q
                pe.wait_ge(ada_summed, n + 1)
                if q == 0:
                    pe.wait_ge(mod_ready, 1)
                for s in range(2):
                    mm = nc.tensor.matmul(bank(4, 2, 2 * (2 * q + s)), ada_acc[n % ACCS][:, P * s:P * (s + 1)], ada_ones[:, 0:2],
                                          start=True, stop=True)
                mm.then_inc(ada_used, 1)
            for g, (a, b) in enumerate(groups):
                pe.wait_ge(z_ready, b)
                for k in range(KD):
                    o = ring_bank(("hT", g, k))
                    for t in range(a, b):
                        mm = nc.tensor.transpose(o[:, (t - a) * P:(t - a + 1) * P], xz[:, t, k * P:(k + 1) * P], ident)
                    mm.then_inc(job_done, 1)
            pe.wait_ge(win_in, 16)
            for i in range(NT):
                if i in (0, 2, 6):
                    g = (0, 2, 6).index(i)
                    job_emptied(pe, ("hT", g, KD - 1))
                    job_emptied(pe, ("hT", g, KD - 2))
                o = ring_bank(("qkv", i))
                lo = QL if i < CT else 0
                for k in range(KD):
                    mm = nc.tensor.matmul(o[:, lo:QKV], hT[:, k, i * P:(i + 1) * P], win[:, k, lo:QKV],
                                          start=k == 0, stop=k == KD - 1)
                mm.then_inc(job_done, 1)
            pe.wait_ge(win2_in, 16)
            cols = {"pool": QKV, "ca": QKV + CW, "cg": QKV + 2 * CW}
            n_mixed = 0
            for name, _ in ring.jobs:
                if name[0] in cols:
                    kind, j, n = name
                    o = ring_bank(name)
                    a = cols[kind] + P * j
                    for k in range(KD):
                        mm = nc.tensor.matmul(o, win[:, k, a:a + P], hT[:, k, CTX + 512 * n:CTX + 512 * (n + 1)],
                                              start=k == 0, stop=k == KD - 1)
                    mm.then_inc(job_done, 1)
                    if n_mixed >= 8:
                        second_cols(2 * (n_mixed - 8))
                        second_cols(2 * (n_mixed - 8) + 1)
                    n_mixed += 1
                elif name[0] == "gate":
                    o = ring_bank(name)
                    n = 4 * name[1] + name[2]
                    pe.wait_ge(ada_summed, n + 1)
                    nc.tensor.matmul(o[:, 0:256], ada_ones, ada_acc[n % ACCS], start=True, stop=True).then_inc(job_done, 1)
            pe.wait_ge(lat_ready, NT)
            for c_ in range(2):
                for n in range(2):
                    o = ring_bank(("qcT", c_, n))
                    for t in range(4):
                        mm = nc.tensor.transpose(o[:, t * P:(t + 1) * P], qkv[:, CT + 4 * n + t, c_ * P:(c_ + 1) * P], ident)
                    mm.then_inc(job_done, 1)
            for kind, lo, m in (("kvT", QL, P), ("krT", QKV - HD, HD)):
                if kind == "krT":
                    pe.wait_ge(kr_ready, 1)
                for g, (a, b) in enumerate(groups):
                    o = ring_bank((kind, g))
                    for t in range(a, b):
                        mm = nc.tensor.transpose(o[0:m, (t - a) * P:(t - a + 1) * P], qkv[:, t, lo:lo + m], ident)
                    mm.then_inc(job_done, 1)
            n_slot = {"a": 0, "b": 0}

            def slot(name, b):
                assert slot_no[name] == (b, n_slot[b] + 1), name
                if n_slot[b]:
                    pe.wait_ge(cleared[b], n_slot[b])
                n_slot[b] += 1
                o = bank(SLOT_BANK[b])
                kind = name[0]
                if kind == "P":
                    _, i, part = name
                    if part == 0:
                        pe.wait_ge(probs_ready, i + 1)
                    for t in range(4 * part, min(4 * part + 4, NT)):
                        mm = nc.tensor.transpose(o[:, (t - 4 * part) * P:(t - 4 * part + 1) * P],
                                                 probs[:, i % 2, t * P:(t + 1) * P], ident)
                elif kind == "q":
                    _, h, n = name
                    for t in range(2):
                        for c_ in range(2):
                            mm = nc.tensor.matmul(o[:, 2 * t * HD:2 * (t + 1) * HD], qcT[:, c_, (2 * n + t) * P:(2 * n + t + 1) * P],
                                                  wuq[:, c_, h * HD:(h + 2) * HD], start=c_ == 0, stop=c_ == 1)
                elif kind in ("qraw", "qrot"):
                    _, h, n = name
                    src = qraw[:, h % 2] if kind == "qraw" else qrot
                    if kind == "qraw":
                        slot_cleared(pe, ("q", h - h % 2, 2 * n + 1))
                    else:
                        pe.wait_ge(rope_ready, h + 1)
                    for t in range(4):
                        mm = nc.tensor.transpose(o[0:HD, t * P:(t + 1) * P], src[:, 4 * n + t, :], ident)
                elif kind == "kn":
                    _, h, n = name
                    w = min(512, KEYS - 512 * n)
                    mm = nc.tensor.matmul(o[0:NOPE, 0:w], wukv[:, h * P:h * P + NOPE], kvT[:, 512 * n:512 * n + w],
                                          start=True, stop=True)
                elif kind == "O":
                    _, p, n = name
                    pe.wait_ge(O_kept, 2 * LT * (p + 1))
                    for t in range(4):
                        mm = nc.tensor.transpose(o[:, t * P:(t + 1) * P], Opair[p % 2][:, 4 * n + t, :], ident)
                elif kind == "pool":
                    _, j, n = name
                    pe.wait_ge(pdif_ready, 2)
                    pe.wait_ge(diag_in, 64)
                    mm = nc.tensor.matmul(o, bdiag[:, j, :], pdif[:, j, 512 * n:512 * (n + 1)], start=True, stop=True)
                elif kind == "y":
                    _, s = name
                    pe.wait_ge(conv_ready, 2 * TAPS)
                    for t in range(2):
                        for j in range(2):
                            mm = nc.tensor.transpose(o[:, (2 * t + j) * P:(2 * t + j + 1) * P],
                                                     yconv[:, j, (2 * s + t) * P:(2 * s + t + 1) * P], ident)
                elif kind == "pw":
                    _, j, n = name
                    pe.wait_ge(pw_in, 16)
                    pe.wait_ge(yact_ready, 1)
                    for k in range(2):
                        mm = nc.tensor.matmul(o, pw[:, k, j * P:(j + 1) * P], yconv[:, k, HALVES[n]], start=k == 0, stop=k == 1)
                elif kind == "yT":
                    _, j, n = name
                    pe.wait_ge(ytok_ready, LT)
                    for t in range(4):
                        mm = nc.tensor.transpose(o[:, t * P:(t + 1) * P], ytok[:, 4 * n + t, j * P:(j + 1) * P], ident)
                mm.then_inc(filled[b], 1)

            pe.wait_ge(wq_in, 32)
            job_emptied(pe, ("kvT", 2))
            wv = wukv.rearrange("p (h e) -> p h e", h=HEADS)[:, :, NOPE:NOPE + VD]
            job_emptied(pe, ("qcT", 1, 0))
            job_emptied(pe, ("qcT", 1, 1))
            for i in range(NT):
                for name, b in first_head(i):
                    slot(name, b)
                o = ring_bank(("V", i))
                nc.tensor.matmul(o, kvT[:, i * P:(i + 1) * P], wv, start=True, stop=True).then_inc(job_done, 1)
            for name, b in first_head(NT):
                slot(name, b)
            pe.wait_ge(emptied["act"], ring.n["act"])
            pe.wait_ge(emptied["dve"], ring.n["dve"])

            def scores(i):
                h, qt = i // LT, i % LT
                if i == LT:
                    pe.wait_ge(odd_rope, 2)
                if qt == 0:
                    for name, _ in prep_slots(h):
                        if name[0] != "q":
                            slot_cleared(pe, name)
                if i >= 2:
                    pe.wait_ge(probs_ready, i - 1)
                qs = slice(qt * P, (qt + 1) * P)
                lat = 0 if i % 2 == 0 else 3
                p = h % 2

                def product(o, rotated, keys):
                    q_hi, q_lo = QT_hi[p][0:HD, rotated, qs], QT_lo[p][0:HD, rotated, qs]
                    k_hi, k_lo = KT_hi[p][0:HD, keys], KT_lo[p][0:HD, keys]
                    nc.tensor.matmul(o, q_hi, k_hi, start=True, stop=False)
                    nc.tensor.matmul(o, q_hi, k_lo, start=False, stop=False)
                    return nc.tensor.matmul(o, q_lo, k_hi, start=False, stop=True)

                for n in range(2):
                    product(bank(lat + n), 1, slice(CTX + 512 * n, CTX + 512 * (n + 1)))
                if i >= 1:
                    pe.wait_ge(probs_ready, i)
                product(bank(2, 256, 256 * (i % 2)), 0, slice(0, CTX)).then_inc(scores_ready, 1)

            def values(i, first, last):
                h = i // LT
                if first == 0:
                    for part in range(3):
                        slot_cleared(pe, ("P", i, part))
                    if i >= 1:
                        pe.wait_ge(O_kept, i)
                for t in range(first, last):
                    key = (t + CT) % NT if i % 2 == 0 else t
                    mm = nc.tensor.matmul(bank(7, VD), probsT[:, i % 2, t, :], V[:, key, h * VD:(h + 1) * VD],
                                          start=t == 0, stop=t == NT - 1)
                if last == NT:
                    mm.then_inc(O_ready, 1)

            for i, named in enumerate(slots_at):
                if i < UNITS:
                    scores(i)
                mine = [s for s in named if s[0][0] == "P"]
                for s in mine[:2]:
                    slot(*s)
                if 2 <= i < UNITS + 2:
                    values(i - 2, 0, 6)
                for s in mine[2:]:
                    slot(*s)
                if 2 <= i < UNITS + 2:
                    values(i - 2, 6, NT)
                for s in named:
                    if s[0][0] != "P":
                        slot(*s)
            stage3_tensor(pe)

        @block.scalar
        def _(act):
            job_emptied(act, ("rows",))
            nc.scalar.activation(sc[:, :], col[:, 0:16], ACT.Silu).then_inc(silu_ready, 1)
            for r in range(4):
                act.wait_ge(ada_used, 2 * r + 2)
                nc.scalar.copy(mrow[0:2, 512 * r:512 * (r + 1)], bank(5 + r % 3)[0:2, :]).then_inc(mod_rows, 1)

            def evac(name, b):
                n = slot_no[name][1]
                act.wait_ge(filled[b], n)
                o = bank(SLOT_BANK[b])
                kind = name[0]
                if kind == "P":
                    _, i, part = name
                    if i >= 2 and part == 0:
                        act.wait_ge(O_ready, i - 1)
                    t0 = 4 * part
                    t1 = min(t0 + 4, NT)
                    ins = nc.scalar.copy(probsT[:, i % 2, t0:t1, :].rearrange("p t q -> p (t q)"), o[:, 0:(t1 - t0) * P])
                elif kind == "q":
                    _, h, m = name
                    if h >= 2:
                        act.wait_ge(rope_ready, h)
                    ins = nc.scalar.copy(qraw[:, :, 2 * m:2 * m + 2, :], o[:, 0:4 * HD].rearrange("p (t h d) -> p h t d", t=2, h=2))
                elif kind == "O":
                    _, p, m = name
                    if p == 0 and m == 0:
                        act.wait_ge(pdif_ready, 2)
                    ins = nc.scalar.copy(mixT[:, p, 512 * m:512 * (m + 1)], o)
                elif kind == "yT":
                    _, j, m = name
                    ins = nc.scalar.activation(yconv[:, j, 512 * m:512 * (m + 1)], o, ACT.Identity,
                                               bias=col[:, R_LB + j:R_LB + j + 1], scale=col[:, R_LG + j:R_LG + j + 1])
                ins.then_inc(cleared[b], 1)

            def first(before):
                for name, b in first_head(before):
                    if b == "a":
                        evac(name, b)

            first_hT = True
            for name, e in ring.jobs:
                if e != "act":
                    continue
                n = ring.of[name][0]
                b = bank(n % 4)
                kind = name[0]
                if kind == "hT" and first_hT:
                    act.wait_ge(mod_ready, 1)
                    first_hT = False
                if kind == "V":
                    first(name[1])
                act.wait_ge(job_done, n + 1)
                if kind == "hT":
                    _, g, k = name
                    a, z = groups[g]
                    w = 0 if g else 1
                    ins = nc.scalar.activation(hT[:, k, a * P:z * P], b[:, 0:(z - a) * P], ACT.Identity,
                                               bias=mod1[:, 0, k, w:w + 1], scale=mod1[:, 1, k, w:w + 1])
                elif kind == "qkv":
                    i = name[1]
                    lo = QL if i < CT else 0
                    ins = nc.scalar.copy(qkv[:, i, lo:QKV], b[:, lo:QKV])
                elif kind == "pool":
                    _, j, m = name
                    act.wait_ge(pads_ready, 1)
                    ins = nc.scalar.copy(upool[:, j, PPAD + 512 * m:PPAD + 512 * (m + 1)], b)
                elif kind == "cg":
                    _, j, m = name
                    at = 2 * j + m
                    if at >= 2:
                        job_emptied(act, ("ca", (at - 2) // 2, (at - 2) % 2))
                    ins = nc.scalar.activation(sig[:, at % 2, :], b, ACT.Sigmoid)
                elif kind == "qcT":
                    _, c_, m = name
                    ins = nc.scalar.activation(qcT[:, c_, 512 * m:512 * (m + 1)], b, ACT.Copy, scale=col[:, R_QG + c_:R_QG + c_ + 1])
                elif kind == "kvT":
                    a, z = groups[name[1]]
                    ins = nc.scalar.activation(kvT[:, a * P:z * P], b[:, 0:(z - a) * P], ACT.Copy, scale=col[:, R_KVG:R_KVG + 1])
                elif kind == "V":
                    ins = nc.scalar.copy(V[:, name[1], :], b)
                ins.then_inc(emptied["act"], 1)
                if name == ("qkv", NT - 2):
                    count = 0
                    act.wait_ge(zeros_ready, 1)
                    for i in range(NT):
                        job_emptied(act, ("qkv", i))
                        for m, lo, w in ((0, 0, QL), (1, QL, KVL)):
                            if m == 0 and i < CT:
                                continue
                            if count:
                                act.wait_ge(ssq_ready, count)
                            nc.scalar.activation(junk[:, 0:w], qkv[:, i, lo:lo + w], ACT.Square,
                                                 accum_out=ssq[:, i, m:m + 1]).then_inc(ssq_ready, 1)
                            count += 1

            first(NT)
            job_emptied(act, ("krT", 2))
            for pair in (KT_hi, KT_lo):
                nc.scalar.copy(pair[1][NOPE:HD, :], pair[0][NOPE:HD, :].bitcast(F32)).then_inc(odd_rope, 1)

            def exp(i):
                act.wait_ge(nmax_ready, i + 1)
                if i >= 2:
                    b, n = slot_no[("P", i - 2, 2)]
                    act.wait_ge(filled[b], n)
                    b, n = slot_no[("P", i - 2, 1)]
                    act.wait_ge(filled[b], n)
                if i >= 4:
                    act.wait_ge(O_kept, i - 3)
                at = KEYS * (i % 2)
                nc.scalar.activation(probs[:, i % 2, :], psum[:, at:at + KEYS], ACT.Exp, bias=nmax[:, 2 + i % 2:3 + i % 2],
                                     scale=SCALE, accum_out=rsum[:, i % 4:i % 4 + 1]).then_inc(probs_ready, 1)

            for i, named in enumerate(slots_at):
                mine = [s for s in named if s[1] == "a"]
                for s in mine:
                    if s[0][0] == "P" and s[0][2] == 0:
                        evac(*s)
                if i < UNITS:
                    exp(i)
                for s in mine:
                    if not (s[0][0] == "P" and s[0][2] == 0):
                        evac(*s)
                if i == TAP_STEP + 14:
                    for j in range(2):
                        slot_cleared(act, ("yT", j, 0))
                        slot_cleared(act, ("yT", j, 1))
                    nc.scalar.activation(yconv, yconv, ACT.Silu).then_inc(yact_ready, 1)
            stage3_scalar(act)

        @block.vector
        def _(dve):
            steps = [0]

            def then(ins):
                chain(dve, dve_step, steps, ins)

            dve.wait_ge(consts_in, 16)
            dve.wait_ge(job_done, 1)
            nc.vector.tensor_copy(col[:, :], bank(0, N_ROWS)).then_inc(emptied["dve"], 1)

            n_z = 0
            for g, (a, b) in enumerate(groups):
                dve.wait_ge(x_in[g], 16)
                for t in range(a, b):
                    for s in range(2):
                        then(nc.vector.bn_stats(stats[:, s, :], xz[:, t, s * 512:(s + 1) * 512]))
                    nc.vector.bn_aggr(mv[:, t, :], stats[:, :, :].rearrange("p a b -> p (a b)")).then_inc(var_ready, 1)
                    dve.wait_ge(var_ready, t + 1)
            for g, (a, b) in enumerate(groups):
                dve.wait_ge(rstd_ready, g + 1)
                for t in range(a, b):
                    nc.vector.tensor_scalar(xz[:, t, :], xz[:, t, :], mv[:, t, 0:1], rstd[:, t:t + 1],
                                            ALU.subtract, ALU.mult).then_inc(z_ready, 1)
            dve.wait_ge(silu_ready, 1)
            dve.wait_ge(mod_sum, 1)
            for w in range(2):
                then(nc.vector.tensor_tensor(mod1[:, :, :, w].rearrange("p a k -> p (a k)"),
                                             bank(4, 32).rearrange("p (k w) -> p k w", w=2)[:, :, w],
                                             col[:, R_MOD1:R_MOD1 + 16], ALU.add))
            nc.vector.tensor_scalar(mod1[:, 1, :, :], mod1[:, 1, :, :], 1.0, None, ALU.add).then_inc(mod_ready, 1)
            dve.wait_ge(mod_ready, 1)

            def two_parts(hi, lo, src):
                then(nc.vector.tensor_copy(hi, src))
                return nc.vector.tensor_tensor(lo, src, hi.bitcast(F32), ALU.subtract)

            taps, summed = [0], [0]

            def sum_piece():
                n = summed[0]
                summed[0] += 1
                dve.wait_ge(ada_in[n % 2], 16 * (n // 2 + 2))
                if n >= ACCS:
                    old = n - ACCS
                    if old < 8:
                        dve.wait_ge(job_done, ring.of[("gate", old // 4, old % 4)][0] + 1)
                    else:
                        dve.wait_ge(ada_used, old + 1)
                w, acc = ada[n % 2], ada_acc[n % ACCS]
                for k in range(KD):
                    if k == 0:
                        ins = nc.vector.tensor_scalar(acc, w[:, k, :], sc[:, k:k + 1], None, ALU.mult)
                    else:
                        ins = nc.vector.scalar_tensor_tensor(acc, w[:, k, :], sc[:, k:k + 1], acc, ALU.mult, ALU.add)
                    if k < KD - 1:
                        then(ins)
                ins.then_inc(ada_summed, 1)

            def tap():
                n = taps[0]
                if n >= 2 * TAPS:
                    return
                taps[0] += 1
                t, j = n // 2, n % 2
                w = col[:, R_DW + n:R_DW + n + 1]
                u = uconv[:, j, t:t + SEQ]
                if t == 0:
                    ins = nc.vector.tensor_scalar(yconv[:, j, :], u, w, col[:, R_CB + j:R_CB + j + 1], ALU.mult, ALU.add)
                else:
                    dve.wait_ge(conv_ready, n - 1)
                    ins = nc.vector.scalar_tensor_tensor(yconv[:, j, :], u, w, yconv[:, j, :], ALU.mult, ALU.add)
                ins.then_inc(conv_ready, 1)

            def evac(name, b):
                n = slot_no[name][1]
                dve.wait_ge(filled[b], n)
                o = bank(SLOT_BANK[b])
                kind = name[0]
                if kind == "P":
                    _, i, part = name
                    if i >= 2:
                        dve.wait_ge(O_ready, i - 1)
                    t0 = 4 * part
                    ins = nc.vector.tensor_copy(probsT[:, i % 2, t0:t0 + 4, :].rearrange("p t q -> p (t q)"), o)
                elif kind in ("qraw", "qrot"):
                    _, h, m = name
                    rot, cols = int(kind == "qrot"), slice(512 * m, 512 * (m + 1))
                    ins = two_parts(QT_hi[h % 2][0:HD, rot, cols], QT_lo[h % 2][0:HD, rot, cols], o[0:HD, :])
                elif kind == "kn":
                    _, h, m = name
                    w = min(512, KEYS - 512 * m)
                    cols = slice(512 * m, 512 * m + w)
                    ins = two_parts(KT_hi[h % 2][0:NOPE, cols], KT_lo[h % 2][0:NOPE, cols], o[0:NOPE, 0:w])
                elif kind == "O":
                    _, p, m = name
                    if p == 0:
                        dve.wait_ge(pdif_ready, 2)
                    ins = nc.vector.tensor_copy(mixT[:, p, 512 * m:512 * (m + 1)], o)
                elif kind == "pool":
                    _, j, m = name
                    ins = nc.vector.tensor_scalar(mixT[:, 4 + j, 512 * m:512 * (m + 1)], o, col[:, R_PSC + j:R_PSC + j + 1],
                                                  None, ALU.mult)
                elif kind == "pw":
                    _, j, m = name
                    ins = nc.vector.tensor_copy(mixT[:, 6 + j, HALVES[m]], o)
                elif kind == "y":
                    s = name[1]
                    ins = nc.vector.tensor_copy(ytok[:, 2 * s:2 * s + 2, :].rearrange("p t c -> p (t c)"), o)
                ins.then_inc(cleared[b], 1)

            def first(before):
                for name, b in first_head(before):
                    if b == "b":
                        evac(name, b)

            for name, e in ring.jobs:
                if e != "dve" or name[0] == "rows":
                    continue
                n = ring.of[name][0]
                b = bank(n % 4)
                kind = name[0]
                dve.wait_ge(job_done, n + 1)
                if kind == "hT":
                    _, g, k = name
                    a, z = groups[g]
                    w = 0 if g else 1
                    ins = nc.vector.tensor_scalar(hT[:, k, a * P:z * P], b[:, 0:(z - a) * P], mod1[:, 1, k, w:w + 1],
                                                  mod1[:, 0, k, w:w + 1], ALU.mult, ALU.add)
                elif kind == "qkv":
                    i = name[1]
                    lo = QL if i < CT else 0
                    ins = nc.vector.tensor_copy(qkv[:, i, lo:QKV], b[:, lo:QKV])
                elif kind == "ca":
                    _, j, m = name
                    job_emptied(dve, ("cg", j, m))
                    ins = nc.vector.tensor_tensor(uconv[:, j, CPAD + 512 * m:CPAD + 512 * (m + 1)], b,
                                                  sig[:, (2 * j + m) % 2, :], ALU.mult)
                elif kind == "gate":
                    _, m, q = name
                    if m == 0 and q == 0:
                        dve.wait_ge(gates_in, 32)
                    g_ = gates[:, m, 256 * q:256 * (q + 1)]
                    ins = nc.vector.tensor_tensor(g_, b[:, 0:256], g_, ALU.add)
                elif kind == "qcT":
                    _, c_, m = name
                    ins = nc.vector.tensor_scalar(qcT[:, c_, 512 * m:512 * (m + 1)], b,
                                                  col[:, R_QG + c_:R_QG + c_ + 1], None, ALU.mult)
                elif kind == "krT":
                    g = name[1]
                    a, z = groups[g]
                    ins = two_parts(KT_hi[0][NOPE:HD, a * P:z * P], KT_lo[0][NOPE:HD, a * P:z * P], b[NOPE:HD, 0:(z - a) * P])
                if ins is not None:
                    ins.then_inc(emptied["dve"], 1)
                if name in (("qkv", 5), ("qkv", 7), ("qkv", 9), ("gate", 0, 0), ("gate", 0, 2)):
                    sum_piece()
                if kind == "gate" or name in (("ca", 0, 0), ("ca", 1, 0)):
                    sum_piece()
                if name == ("ca", 1, 0):
                    sum_piece()
                if name == ("gate", 0, 1):
                    dve.wait_ge(rq_ready, 1)
                    for i in range(NT):
                        if i >= CT:
                            then(nc.vector.tensor_scalar(qkv[:, i, 0:QL], qkv[:, i, 0:QL], rq[:, i, 0:1], None, ALU.mult))
                        nc.vector.tensor_scalar(qkv[:, i, QL:QL + KVL], qkv[:, i, QL:QL + KVL], rq[:, i, 1:2], None,
                                                ALU.mult).then_inc(lat_ready, 1)
                if name == ("krT", 2):
                    dve.wait_ge(ada_used, 16)
                    then(nc.vector.tensor_tensor(mod2[:, :, :].rearrange("p a k -> p (a k)"),
                                                 bank(4, 32).rearrange("p (k w) -> p k w", w=2)[:, :, 0],
                                                 col[:, R_MOD2:R_MOD2 + 16], ALU.add))
                    nc.vector.tensor_scalar(mod2[:, 1, :], mod2[:, 1, :], 1.0, None, ALU.add).then_inc(mod_ready, 1)
                    job_emptied(dve, ("ca", 1, 1))
                    dve.wait_ge(zeros_ready, 1)

            for before in range(NT + 1):
                first(before)

            for _ in range(TAP_FIRST):
                tap()
            for i, named in enumerate(slots_at):
                if i < UNITS:
                    dve.wait_ge(scores_ready, i + 1)
                    at = KEYS * (i % 2)
                    m = i % 2
                    if i >= 2:
                        dve.wait_ge(probs_ready, i - 1)
                    then(nc.vector.tensor_reduce(nmax[:, m:m + 1], psum[:, at:at + KEYS], AX.X, ALU.max))
                    nc.vector.tensor_scalar(nmax[:, 2 + m:3 + m], nmax[:, m:m + 1], -SCALE, None,
                                            ALU.mult).then_inc(nmax_ready, 1)
                want = min(2 * TAPS, TAP_FIRST + (2 * TAPS - TAP_FIRST) * (i + 1) // TAP_STEP)
                for s in named:
                    if s[1] == "b" and s[0][0] == "P":
                        evac(*s)
                while taps[0] < want:
                    tap()
                if 2 <= i < UNITS + 2:
                    u = i - 2
                    h, qt, m = u // LT, u % LT, u % 2
                    dve.wait_ge(probs_ready, u + 1)
                    then(nc.vector.reciprocal(rinv[:, m:m + 1], rsum[:, u % 4:u % 4 + 1]))
                    dve.wait_ge(O_ready, u + 1)
                    if h % 2 == 0 and h >= 4 and qt == 0:
                        slot_cleared(dve, ("O", h // 2 - 2, 0))
                        slot_cleared(dve, ("O", h // 2 - 2, 1))
                    nc.vector.tensor_scalar(Opair[(h // 2) % 2][:, qt, VD * (h % 2):VD * (h % 2 + 1)], bank(7, VD),
                                            rinv[:, m:m + 1], None, ALU.mult).then_inc(O_kept, 1)
                for s in named:
                    if s[1] == "b" and s[0][0] != "P":
                        evac(*s)
                if TAP_STEP + 4 < i <= TAP_STEP + 4 + 4:
                    s = i - TAP_STEP - 5
                    slot_cleared(dve, ("y", s))
                    for t in (2 * s, 2 * s + 1):
                        then(nc.vector.bn_stats(stats[:, 0, :], ytok[:, t, :]))
                        nc.vector.bn_aggr(mv[:, t, :], stats[:, 0, :]).then_inc(var_ready, 1)
                        dve.wait_ge(var_ready, NT + t + 1)
                if TAP_STEP + 9 <= i <= TAP_STEP + 10:
                    dve.wait_ge(rstd_ready, 4)
                    a = 4 * (i - TAP_STEP - 9)
                    for t in range(a, a + 4):
                        nc.vector.tensor_scalar(ytok[:, t, :], ytok[:, t, :], mv[:, t, 0:1], rstd[:, t:t + 1],
                                                ALU.subtract, ALU.mult).then_inc(ytok_ready, 1)
            stage3_vector(dve, then)

        @block.gpsimd
        def _(pool):
            steps = [0]

            def then(ins):
                chain(pool, pool_step, steps, ins)

            def inv_root(dst, src, scale):
                then(nc.gpsimd.tensor_scalar(dst, src, scale, EPS, ALU.mult, ALU.add))
                return nc.gpsimd.tensor_tensor(dst, dst, mhalf_like(dst), ALU.pow)

            def mhalf_like(dst):
                n = 1
                for d in dst.shape[1:]:
                    n *= d
                v = mhalf[:, 0:n]
                return v if len(dst.shape) == 2 else v.rearrange("p (a b) -> p a b", b=dst.shape[2])

            then(nc.gpsimd.memset(mhalf[:, :], -0.5))
            then(nc.gpsimd.memset(ssq[:, :, :], 1.0))
            nc.gpsimd.memset(ada_ones, 1.0)
            nc.gpsimd.memset(bdiag[:, :, :], 0.0)
            nc.gpsimd.memset(uconv[:, :, 0:CPAD], 0.0)
            nc.gpsimd.memset(uconv[:, :, CPAD + SEQ:], 0.0).then_inc(zeros_ready, 1)
            for g, (a, b) in enumerate(groups):
                pool.wait_ge(var_ready, b)
                inv_root(rstd[:, a:b], mv[:, a:b, 1], 1.0).then_inc(rstd_ready, 1)
            pool.wait_ge(job_done, ring.of[("hT", 2, KD - 1)][0] + 1)
            nc.gpsimd.memset(upool[:, :, 0:PPAD], 0.0)
            nc.gpsimd.memset(upool[:, :, PPAD + SEQ:], 0.0).then_inc(pads_ready, 1)
            pool.wait_ge(ssq_ready, NT + LT)
            then(nc.gpsimd.tensor_scalar(rq[:, :, 0], ssq[:, :, 0], 1.0 / QL, EPS, ALU.mult, ALU.add))
            then(nc.gpsimd.tensor_scalar(rq[:, :, 1], ssq[:, :, 1], 1.0 / KVL, EPS, ALU.mult, ALU.add))
            nc.gpsimd.tensor_tensor(rq[:, :, :], rq[:, :, :], mhalf_like(rq[:, :, :]), ALU.pow).then_inc(rq_ready, 1)

            cos = cst[:, C_COS:C_COS + 128].rearrange("p (t a f) -> p t a f", t=LT, a=2)
            sin = cst[:, C_SIN:C_SIN + 128].rearrange("p (t a f) -> p t a f", t=LT, a=2)

            def rotate(src, dst):
                s = src.rearrange("p t (a m f) -> p t a m f", a=2, m=2)
                d = dst.rearrange("p t (a m f) -> p t a m f", a=2, m=2)
                x1, x2 = s[:, :, :, 0, :], s[:, :, :, 1, :]
                tm = [rtmp[:, n, :].rearrange("p (t a f) -> p t a f", t=LT, a=2) for n in range(4)]
                nc.gpsimd.tensor_tensor(tm[0], x1, cos, ALU.mult)
                nc.gpsimd.tensor_tensor(tm[1], x2, sin, ALU.mult)
                nc.gpsimd.tensor_tensor(tm[2], x2, cos, ALU.mult)
                then(nc.gpsimd.tensor_tensor(tm[3], x1, sin, ALU.mult))
                nc.gpsimd.tensor_tensor(d[:, :, :, 0, :], tm[0], tm[1], ALU.subtract)
                return nc.gpsimd.tensor_tensor(d[:, :, :, 1, :], tm[2], tm[3], ALU.add)

            kr = qkv[:, CT:NT, QL + KVL:QKV]
            rotate(kr, kr).then_inc(kr_ready, 1)
            pool.wait_ge(kr_ready, 1)

            def rope_q(h):
                slot_cleared(pool, ("q", h - h % 2, 3))
                if h >= 1:
                    slot_filled(pool, ("qrot", h - 1, 0))
                    slot_filled(pool, ("qrot", h - 1, 1))
                nc.gpsimd.tensor_copy(qrot[:, :, 0:NOPE], qraw[:, h % 2, :, 0:NOPE])
                rotate(qraw[:, h % 2, :, NOPE:HD], qrot[:, :, NOPE:HD]).then_inc(rope_ready, 1)
                pool.wait_ge(rope_ready, h + 1)

            def slot_filled(eng, name):
                b, n = slot_no[name]
                eng.wait_ge(filled[b], n)

            rope_q(0)
            for j in range(2):
                for m in range(2):
                    job_emptied(pool, ("pool", j, m))
            W = SEQ + 2 * PPAD
            for j in range(2):
                src, width = upool[:, j, :], W
                for d in range(2 * j + 2):
                    step = 1 << d
                    width -= step
                    half = slice(0, P) if d <= 2 * j else slice(PG, P)
                    dst = ptmp[:, d % 2, :]
                    then(nc.gpsimd.tensor_tensor(dst[half, 0:width], src[half, 0:width],
                                                 src[half, step:step + width], ALU.add))
                    w = step * 2
                    for s in range(2):
                        if POOL_W[2 * j + s] == w:
                            rows_ = slice(PG * s, PG * (s + 1))
                            o = PPAD - w // 2
                            then(nc.gpsimd.tensor_scalar(pdif[rows_, j, :], dst[rows_, o:o + SEQ],
                                                         cst[rows_, C_WINV + j:C_WINV + j + 1], None, ALU.mult))
                    src = dst
                e = cst[:, C_EDGE + 16 * j:C_EDGE + 16 * (j + 1)]
                then(nc.gpsimd.tensor_tensor(pdif[:, j, 0:PPAD], pdif[:, j, 0:PPAD], e[:, 0:PPAD], ALU.mult))
                then(nc.gpsimd.tensor_tensor(pdif[:, j, SEQ - PPAD:SEQ], pdif[:, j, SEQ - PPAD:SEQ],
                                             e[:, PPAD:16], ALU.mult))
                nc.gpsimd.tensor_tensor(pdif[:, j, :], pdif[:, j, :], upool[:, j, PPAD:PPAD + SEQ], ALU.subtract)\
                    .then_inc(pdif_ready, 1)
            for h in range(1, HEADS):
                rope_q(h)
                if h == (TAP_STEP + 12) // LT:
                    pool.wait_ge(var_ready, NT + LT)
                    inv_root(rstd[:, 0:LT], mv[:, 0:LT, 1], 1.0).then_inc(rstd_ready, 1)
            stage3_gpsimd(pool, then)


NAMES = ("x", "c", "ctx", "c_ctx", "ada_w", "ada_b", "w_in", "q_norm_g", "w_uq", "kv_norm_g", "w_ukv", "pool_w",
         "pool_scale", "conv_dw", "conv_b", "conv_ln_g", "conv_ln_b", "conv_pw", "w_out", "ln1_g", "ln1_b",
         "router_w", "router_bias", "exp_wg", "exp_wu", "exp_wd", "sh_wg", "sh_wu", "sh_wd", "ln2_g", "ln2_b")
LAYERED = NAMES[4:]


def kernel(**inputs):
    from concourse import bacc
    from concourse.bass_utils import run_bass_kernel_spmd

    nc = bacc.Bacc("TRN2", target_bir_lowering=False, num_devices=1)
    arrays = {}
    for name in NAMES:
        a = np.asarray(inputs[name])
        arrays[name] = np.ascontiguousarray(a[0] if name in LAYERED else a)
    arrays["const"] = shape_constants()
    arrays["zero_rows"] = np.zeros((P, D), np.float32)
    args = {n: nc.dram_tensor("in_" + n, a.shape, F32, kind="ExternalInput").ap() for n, a in arrays.items()}
    out = nc.dram_tensor("out_rows", (1, SEQ, D), F32, kind="ExternalOutput").ap()
    build(nc, out=out, **args)
    r = run_bass_kernel_spmd(nc, [{"in_" + n: a for n, a in arrays.items()}], core_ids=[0])
    return r.results[0]["out_rows"]
```
